# Optimizing a Trainium2 kernel written in Bass

```python
import jax, jax.numpy as jnp
from jax import lax
import numpy as np

D_MODEL = 1024
BATCH = 1
SEQ = 1024
DEPTH = 1

GDN_HEADS = 4
GDN_DK = 128
GDN_DV = 128
GDN_CONV = 4
GDN_CHUNK = 64
HG_HEADS = 4
HG_DF = 128
HG_DI = 128
HG_CHUNK = 16
N_BRANCH = 2
NORM_EPS = 1e-6

GDN_QK = GDN_HEADS * GDN_DK
GDN_V = GDN_HEADS * GDN_DV
HG_F = HG_HEADS * HG_DF
HG_I = HG_HEADS * HG_DI
SPLIT_SIZES = [2 * GDN_QK + GDN_V,
               GDN_HEADS,
               GDN_HEADS,
               GDN_V,
               HG_F,
               HG_F,
               HG_I,
               HG_I,
               N_BRANCH * D_MODEL]
IN_COLS = sum(SPLIT_SIZES)
SPLIT_IDX = [int(v) for v in np.cumsum(SPLIT_SIZES)[:-1]]

kernel_name = "hybrid_gdn_hgrn2_gated_merge"

def _rmsnorm(x, w):
    xf = x.astype(jnp.float32)
    y = xf * lax.rsqrt(jnp.mean(xf * xf, axis=-1, keepdims=True) + NORM_EPS)
    return (y * w.astype(jnp.float32)).astype(x.dtype)

def _l2norm(t):
    t = t.astype(jnp.float32)
    return t * lax.rsqrt(jnp.sum(t * t, axis=-1, keepdims=True) + NORM_EPS)

def _causal_depthwise_conv(x, w):
    k = w.shape[0]
    return lax.conv_general_dilated(
        x, w[:, None, :].astype(x.dtype), window_strides=(1,), padding=[(k - 1, 0)],
        dimension_numbers=("NWC", "WIO", "NWC"), feature_group_count=x.shape[-1])

def _masked_exp(diff, mask):
    return jnp.where(mask, jnp.exp(jnp.where(mask, diff, 0.0)), 0.0)

def _to_chunks(t, c):
    b, s, h = t.shape[:3]
    t = t.reshape((b, s // c, c, h) + t.shape[3:])
    return t.transpose((1, 0, 3, 2) + tuple(range(4, t.ndim)))

def _from_chunks(t):
    n, b, h, c = t.shape[:4]
    t = t.transpose((1, 0, 3, 2) + tuple(range(4, t.ndim)))
    return t.reshape((b, n * c, h) + t.shape[4:])

def _gated_delta_rule(q, k, v, g, beta):
    f32 = jnp.float32
    c = GDN_CHUNK
    dk, dv = q.shape[-1], v.shape[-1]
    q, k, v, g, beta = (_to_chunks(t.astype(f32), c) for t in (q, k, v, g, beta))
    G = jnp.cumsum(g, axis=-1)
    causal = jnp.tril(jnp.ones((c, c), bool))
    strict = jnp.tril(jnp.ones((c, c), bool), -1)
    L = _masked_exp(G[..., :, None] - G[..., None, :], causal)
    kb = k * beta[..., None]
    A = jnp.where(strict, jnp.einsum("nbhid,nbhjd->nbhij", kb, k) * L, 0.0)
    M = A + jnp.eye(c, dtype=f32)
    rhs = jnp.concatenate([v * beta[..., None], kb * jnp.exp(G)[..., None]], axis=-1)
    sol = lax.linalg.triangular_solve(M, rhs, left_side=True, lower=True, unit_diagonal=True)
    u, w = sol[..., :dv], sol[..., dv:]
    qs = q * (dk ** -0.5)
    a_qk = jnp.einsum("nbhid,nbhjd->nbhij", qs, k) * L
    qg = qs * jnp.exp(G)[..., None]
    kdec = k * jnp.exp(G[..., -1:] - G)[..., None]
    gl = jnp.exp(G[..., -1])

    def step(S, inp):
        u_c, w_c, qg_c, a_c, kd_c, gl_c = inp
        v_new = u_c - jnp.einsum("bhck,bhkv->bhcv", w_c, S)
        o = jnp.einsum("bhck,bhkv->bhcv", qg_c, S) + jnp.einsum("bhij,bhjv->bhiv", a_c, v_new)
        S = gl_c[..., None, None] * S + jnp.einsum("bhck,bhcv->bhkv", kd_c, v_new)
        return S, o

    S0 = jnp.zeros(q.shape[1:3] + (dk, dv), f32)
    _, o = lax.scan(step, S0, (u, w, qg, a_qk, kdec, gl))
    return _from_chunks(o)

def _hgrn2_chunked(q, k, v, log_f):
    f32 = jnp.float32
    c = HG_CHUNK
    q, k, v, log_f = (_to_chunks(t.astype(f32), c) for t in (q, k, v, log_f))
    G = jnp.cumsum(log_f, axis=-2)
    qg = q * jnp.exp(G)
    kdec = k * jnp.exp(G[..., -1:, :] - G)
    gl = jnp.exp(G[..., -1, :])
    causal = jnp.tril(jnp.ones((c, c), bool))[:, :, None]

    def step(S, inp):
        q_c, k_c, G_c, v_c, qg_c, kd_c, gl_c = inp
        D = _masked_exp(G_c[..., :, None, :] - G_c[..., None, :, :], causal)
        a = jnp.einsum("bhif,bhjf,bhijf->bhij", q_c, k_c, D)
        o = jnp.einsum("bhij,bhjv->bhiv", a, v_c) + jnp.einsum("bhcf,bhfv->bhcv", qg_c, S)
        S = gl_c[..., :, None] * S + jnp.einsum("bhcf,bhcv->bhfv", kd_c, v_c)
        return S, o

    S0 = jnp.zeros(q.shape[1:3] + (q.shape[-1], v.shape[-1]), f32)
    _, o = lax.scan(step, S0, (q, k, G, v, qg, kdec, gl))
    return _from_chunks(o)

def setup_inputs(seed: int = 0) -> dict:
    key = jax.random.key(seed)
    ks = jax.random.split(key, 12)
    f32 = jnp.float32
    x = jax.random.normal(ks[0], (BATCH, SEQ, D_MODEL), f32)
    norm_w = 1.0 + 0.02 * jax.random.normal(ks[1], (DEPTH, D_MODEL), f32)
    w_in = jax.random.normal(ks[2], (DEPTH, D_MODEL, IN_COLS), f32) * D_MODEL ** -0.5
    conv_w = jax.random.normal(ks[3], (DEPTH, GDN_CONV, 2 * GDN_QK + GDN_V), f32) * GDN_CONV ** -0.5
    a_log = jnp.log(jax.random.uniform(ks[4], (DEPTH, GDN_HEADS), f32, 1.0, 16.0))
    dt = jnp.exp(jax.random.uniform(ks[5], (DEPTH, GDN_HEADS), f32, np.log(1e-3), np.log(1e-1)))
    dt_bias = dt + jnp.log(-jnp.expm1(-dt))
    gdn_norm_w = 1.0 + 0.02 * jax.random.normal(ks[6], (DEPTH, GDN_DV), f32)
    hg_lb_logits = 0.1 * jax.random.normal(ks[7], (DEPTH, HG_F), f32)
    hg_norm_w = 1.0 + 0.02 * jax.random.normal(ks[8], (DEPTH, HG_DI), f32)
    w_branch = jax.random.normal(ks[9], (DEPTH, N_BRANCH, GDN_V, D_MODEL), f32) * GDN_V ** -0.5
    w_out = jax.random.normal(ks[10], (DEPTH, D_MODEL, D_MODEL), f32) * D_MODEL ** -0.5
    final_norm_w = 1.0 + 0.02 * jax.random.normal(ks[11], (D_MODEL,), f32)
    return {"x": x, "norm_w": norm_w, "w_in": w_in, "conv_w": conv_w, "a_log": a_log,
            "dt_bias": dt_bias, "gdn_norm_w": gdn_norm_w, "hg_lb_logits": hg_lb_logits,
            "hg_norm_w": hg_norm_w, "w_branch": w_branch, "w_out": w_out,
            "final_norm_w": final_norm_w}

def reference(x, norm_w, w_in, conv_w, a_log, dt_bias, gdn_norm_w, hg_lb_logits,
              hg_norm_w, w_branch, w_out, final_norm_w):
    f32 = jnp.float32
    b, s, _ = x.shape
    lb_p = jax.nn.softmax(hg_lb_logits.astype(f32), axis=0)
    lower_bounds = jnp.cumsum(lb_p, axis=0) - lb_p[0]
    h = x
    for l in range(DEPTH):
        xn = _rmsnorm(h, norm_w[l])
        proj = jnp.einsum("bsd,dc->bsc", xn, w_in[l])
        qkv, a_in, b_in, z_a, hq, hf, hi, z_b, gate = jnp.split(proj, SPLIT_IDX, axis=-1)

        qkv = jax.nn.silu(_causal_depthwise_conv(qkv, conv_w[l]))
        q, k, v = jnp.split(qkv, [GDN_QK, 2 * GDN_QK], axis=-1)
        q = _l2norm(q.reshape(b, s, GDN_HEADS, GDN_DK))
        k = _l2norm(k.reshape(b, s, GDN_HEADS, GDN_DK))
        v = v.reshape(b, s, GDN_HEADS, GDN_DV)
        g = -jnp.exp(a_log[l].astype(f32)) * jax.nn.softplus(a_in.astype(f32) + dt_bias[l].astype(f32))
        beta = jax.nn.sigmoid(b_in.astype(f32))
        o_a = _gated_delta_rule(q, k, v, g, beta)
        y_a = _rmsnorm(o_a, gdn_norm_w[l]) * jax.nn.silu(z_a.astype(f32).reshape(b, s, GDN_HEADS, GDN_DV))
        y_a = y_a.reshape(b, s, GDN_V).astype(x.dtype)

        lb = lower_bounds[l].reshape(HG_HEADS, HG_DF)
        f_logit = hf.astype(f32).reshape(b, s, HG_HEADS, HG_DF)
        f_gate = lb + (1.0 - lb) * jax.nn.sigmoid(f_logit)
        log_f = jnp.log(f_gate)
        k_h = (1.0 - lb) * jax.nn.sigmoid(-f_logit)
        o_b = _hgrn2_chunked(hq.reshape(b, s, HG_HEADS, HG_DF), k_h,
                             hi.reshape(b, s, HG_HEADS, HG_DI), log_f)
        y_b = _rmsnorm(o_b, hg_norm_w[l]) * jax.nn.silu(z_b.astype(f32).reshape(b, s, HG_HEADS, HG_DI))
        y_b = y_b.reshape(b, s, HG_I).astype(x.dtype)

        gate_a, gate_b = jnp.split(gate, 2, axis=-1)
        merged = (jax.nn.sigmoid(gate_a) * jnp.einsum("bsw,wd->bsd", y_a, w_branch[l, 0])
                  + jax.nn.sigmoid(gate_b) * jnp.einsum("bsw,wd->bsd", y_b, w_branch[l, 1]))
        h = h + jnp.einsum("bsd,de->bse", merged, w_out[l])
    return _rmsnorm(h, final_norm_w)


_drawn_inputs = setup_inputs


def setup_inputs(seed=0):
    import zlib

    import numpy as np

    out = dict(_drawn_inputs(seed))
    spreads = {}
    factors = {'norm_w': 3.095, 'gdn_norm_w': 8.0, 'hg_norm_w': 8.0, 'final_norm_w': 2.827}
    for name, (base, spread) in spreads.items():
        noise = np.random.default_rng([zlib.crc32(name.encode()), seed]).standard_normal(out[name].shape)
        drawn = base * np.exp(spread * noise) if base else spread * noise
        out[name] = __import__('jax').numpy.asarray(drawn.astype(out[name].dtype))
    for name, factor in factors.items():
        out[name] = (out[name] * factor).astype(out[name].dtype)
    return out
```

```python
from contextlib import ExitStack

import concourse.bass as bass
from concourse import mybir

F32 = mybir.dt.float32
F32R = mybir.dt.float32r
I32 = mybir.dt.int32
ALU = mybir.AluOpType
ACT = mybir.ActivationFunctionType

P = 128
TOK = 1024
DM = 1024
NT = TOK // P
KS = DM // P
H = 4
HALF = 512
EPS = 1e-6
LV = 7
QSCALE = float(P) ** -0.5
MM = 3 * KS

S_AB, S_QKV, S_HQF, S_HI, S_ZA, S_ZB, S_MERGE = 0, 1, 13, 21, 25, 29, 33
S_OUT = S_MERGE + 3 * KS
NS = S_OUT + KS
RING = 3


def first_group(s):
    if s < S_MERGE:
        return 2 * s
    d, r = divmod(s - S_MERGE, 3)
    return 2 * S_MERGE + 8 * d + 2 * r


def end_group(s):
    return first_group(s + 1)


ALL_GROUPS = first_group(S_OUT)


def bass_hybrid_gdn_hgrn2(nc, xT, xtok, w_tiles, params, fnorm, consts, out):
    with ExitStack() as ctx:
        def place(name, shape, dt, offset):
            return nc.alloc_sbuf_tensor_at(name, shape, dt, offset=offset)

        def stack(top):
            def sb(name, shape, dt=F32):
                size = 4
                for n in shape[1:]:
                    size *= n
                t = place(name, shape, dt, top[0])
                top[0] += (size + 31) // 32 * 32
                return t
            return sb

        def sem(name):
            return ctx.enter_context(nc.semaphore(name))

        top = [(nc.sbuf_base + 31) // 32 * 32]
        sb = stack(top)
        xhi = sb("xhi", [P, KS, TOK], F32R)
        xlo = sb("xlo", [P, KS, TOK], F32R)
        ring0 = top[0]
        whi = [sb(f"whi{i}", [P, KS, P], F32R) for i in range(RING)]
        wlo = [sb(f"wlo{i}", [P, KS, P], F32R) for i in range(RING)]
        wraw = [sb(f"wraw{i}", [P, KS, P]) for i in range(2)]
        rms0 = top[0]
        rms = sb("rms", [P, TOK])
        cst = sb("cst", [P, 2 * P + 2 * LV * 64])
        ones = sb("ones", [P, P])
        prm = sb("prm", [P, 64])
        gb_col = sb("gb_col", [P, NT, 64])
        col = sb("col", [P, 64])
        ident, tri = cst[:, 0:P], cst[:, P:2 * P]
        inv_mask = cst[:, 2 * P:2 * P + LV * 64].rearrange("p (l n) -> p l n", l=LV)
        hg_mask = cst[:, 2 * P + LV * 64:2 * P + 2 * LV * 64].rearrange("p (l n) -> p l n", l=LV)
        nw, cw = prm[:, 0:KS], prm[:, 8:56].rearrange("p (c j) -> p c j", j=4)
        gnw, hnw, lbl = prm[:, 56:57], prm[:, 57:58], prm[:, 58:62]
        alog, dtb = prm[0:H, 62:63], prm[0:H, 63:64]
        eps, one = col[:, 0:1], col[:, 1:2]
        nega = col[0:H, 2:3]
        lb, omlb, lbe = col[:, 4:8], col[:, 8:12], col[:, 16:20]
        gcs, gle, kdc = col[:, 12:16], col[:, 16:20], col[:, 20:24]
        ssh, rh = col[:, 24:40].rearrange("p (t e) -> p t e", e=2), col[:, 40:48]

        arena = top[0]
        SLOT = 3 * HALF * 4
        X = place("X", [P, 9, 3 * HALF], F32, arena)
        xraw = place("xraw", [P, KS, TOK], F32, arena)
        work = arena + 56 * 1024

        w1 = [work]
        sb = stack(w1)
        pre = sb("pre", [P, 3 + TOK])
        conv = [sb(f"conv{i}", [P, HALF]) for i in range(2)]
        sqx = [sb(f"sqx{i}", [P, TOK]) for i in range(2)]
        ab = sb("ab", [64, TOK])
        ab1 = sb("ab1", [H, TOK])
        ab2 = sb("ab2", [H, TOK])
        gb = sb("gb", [64, TOK])

        w2 = [work]
        sb = stack(w2)
        sq = sb("sq", [P, 2, HALF])
        kgT, qgT = sq[:, 0, :], sq[:, 1, :]
        kdec = sb("kdec", [P, H, P])
        vtok = sb("vtok", [P, HALF])
        dec = sb("dec", [P, H, P])
        decm = sb("decm", [P, H, P])
        egr = sb("egr", [P, H, P])
        AT = sb("AT", [P, H, P])
        QK = sb("QK", [P, H, P])
        T = sb("T", [P, H, P])
        TT = sb("TT", [P, H, P])
        X0 = sb("X0", [P, HALF])
        vnew = sb("vnew", [P, H, P])
        S = sb("S", [P, H, P])
        U = [sb(f"U{i}", [P, H, P]) for i in range(LV)]

        w3 = [work]
        sb = stack(w3)
        hitok = sb("hitok", [P, NT, H, P])
        w3b = [w3[0]]
        hst = [sb(f"hst{i}", [P, HALF]) for i in range(2)]
        nrm = sb("nrm", [P, HALF])
        sb = stack(w3b)
        QP = sb("QP", [P, H, P])
        KR = sb("KR", [P, H, P])
        FF = sb("FF", [P, H, P])
        TOT = sb("TOT", [P, H * P])
        HA = sb("HA", [P, H, P])
        kdt = sb("kdt", [P, H, P])
        HS = sb("HS", [P, H, P])
        zr = [sb(f"zr{i}", [P, HALF]) for i in range(2)]
        sg = [sb(f"sg{i}", [P, HALF]) for i in range(2)]

        yhi = [place("yahi", [P, H, TOK], F32R, work), place("ybhi", [P, H, TOK], F32R, arena + 4 * SLOT)]
        ylo = [place("yalo", [P, H, TOK], F32R, work + 16384),
               place("yblo", [P, H, TOK], F32R, arena + 4 * SLOT + 16384)]
        mat = [work + 32768, work + 36864] + [arena + 4096 * d for d in range(6)]
        merged = [place(f"merged{d}", [P, TOK], F32, mat[d]) for d in range(KS)]
        gateb = place("gateb", [P, TOK], F32, work + 40960)

        wohi = place("wohi", [P, KS, DM], F32R, work)
        wolo = place("wolo", [P, KS, DM], F32R, arena + 4 * SLOT)
        hat = [ring0 + 4096 * t for t in range(6)] + [rms0, work + 40960]
        hres = [place(f"hres{t}", [P, DM], F32, hat[t]) for t in range(NT)]
        scr = place("scr", [P, DM], F32, arena)
        fnw = place("fnw", [P, DM], F32, arena + 4096)
        assert max(w1[0], w2[0], w3b[0], work + 45056) <= nc.sbuf_usable_end

        B = [ctx.enter_context(nc.psum_tensor(f"bank{i}", [P, HALF], F32)) for i in range(8)]

        s_prm, s_cst, s_fn = sem("s_prm"), sem("s_cst"), sem("s_fn")
        s_x = [sem(f"x_landed{k}") for k in range(KS)]
        s_w = [sem("w_landed0"), sem("w_landed1")]
        s_res = [sem(f"res_landed{t}") for t in range(NT)]
        x_sq, x_hi, x_lo = sem("x_sq"), sem("x_hi"), sem("x_lo")
        ss_done, rms_done = sem("ss_done"), sem("rms_done")
        w_hi, w_lo = sem("w_hi"), sem("w_lo")
        acc_done = sem("acc_done")
        acc_out = [sem("acc_out0"), sem("acc_out1")]
        phase = sem("phase")
        setup = sem("setup")
        dstep, astep, pstep = sem("dstep"), sem("astep"), sem("pstep")
        tap_done, conv_done, silu_done = sem("tap_done"), sem("conv_done"), sem("silu_done")
        ab_row, ab_act, gb_row, gb_turned = sem("ab_row"), sem("ab_act"), sem("gb_row"), sem("gb_turned")
        sq_done, ssq_done, rs_done, qk_norm = sem("sq_done"), sem("ssq_done"), sem("rs_done"), sem("qk_norm")
        gcum_done, dif_done, kv_turned, att_done = (
            sem("gcum_done"), sem("dif_done"), sem("kv_turned"), sem("att_done"))
        dec_done, egr_done, kdc_done, v_out = sem("dec_done"), sem("egr_done"), sem("kdc_done"), sem("v_out")
        decm_done, kg_done = sem("decm_done"), sem("kg_done")
        a_ready, u_psum, u_ready, t_psum, t_ready = (
            sem("a_ready"), sem("u_psum"), sem("u_ready"), sem("t_psum"), sem("t_ready"))
        kd_ready = sem("kd_ready")
        ks_done, x0_done, tx_done, vn_done = sem("ks_done"), sem("x0_done"), sem("tx_done"), sem("vn_done")
        o_done, su_done, s_ready, oa_out = sem("o_done"), sem("su_done"), sem("s_ready"), sem("oa_out")
        hi_turned, hi_out = sem("hi_turned"), sem("hi_out")
        o_sq, o_ss, o_rs, o_nrm = sem("o_sq"), sem("o_ss"), sem("o_rs"), sem("o_nrm")
        hf_sig, hf_f, hk_lb, qf_done = sem("hf_sig"), sem("hf_f"), sem("hk_lb"), sem("qf_done")
        hl_psum, hl_upd, ha_done = sem("hl_psum"), sem("hl_upd"), sem("ha_done")
        hk_turned, hk_out, ho_done, hs_done, hs_ready, ob_out = (
            sem("hk_turned"), sem("hk_out"), sem("ho_done"), sem("hs_done"), sem("hs_ready"), sem("ob_out"))
        z_sig, z_y = sem("z_sig"), sem("z_y")
        y_hi, y_lo = sem("y_hi"), sem("y_lo")
        g_sig, m_done = sem("g_sig"), sem("m_done")
        m_hi, m_lo = sem("m_hi"), sem("m_lo")
        out_done, h_res, h_rs, h_out = sem("out_done"), sem("h_res"), sem("h_rs"), sem("h_out")
        stored = sem("stored")

        def rows(t):
            return slice(P * t, P * (t + 1))

        def qkv(t):
            return X[:, t + 1, :].rearrange("p (c n) -> p c n", n=P)

        def blocks(ap, s):
            return ap.rearrange("p h (b e s) -> p (h b) e s", e=2, s=s)

        def packed(ap, s):
            return ap.rearrange("p (b s) -> p b s", s=s)

        def mask(m, lv):
            s = 1 << lv
            return m[:, lv, :].rearrange("p (b s) -> p b s", s=s)[:, None, :, :].broadcast_to([P, H, 64 // s, s])

        def by_head(ap):
            return ap[:, :, None].broadcast_to([P, H, P])

        def totals(lv):
            if lv == 0:
                tot = FF[:].rearrange("p h n -> p (h n)")
            else:
                at = sum(H * P >> i for i in range(1, lv))
                tot = TOT[:, at:at + (H * P >> lv)]
            return tot.rearrange("p (b e) -> p b e", e=2)

        def out_of_bank(eng, g):
            eng.wait_ge(acc_out[g % 2], g // 2 + 1)

        def leave(eng):
            eng.drain().then_inc(phase, 1)

        def enter(eng, n):
            eng.wait_ge(phase, 4 * n)

        block = ctx.enter_context(nc.Block())

        @block.sync
        def _(sp):
            def load_w(s):
                if s >= 2:
                    sp.wait_ge(w_hi, s - 1)
                    sp.wait_ge(w_lo, s - 1)
                sp.dma_start(wraw[s % 2][:].rearrange("p k n -> p (k n)"), w_tiles[s]).then_inc(s_w[s % 2], 16)

            sp.dma_start(prm[:], params).then_inc(s_prm, 16)
            sp.dma_start(xraw[:, 0, :], xT[0:P, :]).then_inc(s_x[0], 16)
            load_w(0)
            for k in range(1, KS):
                sp.dma_start(xraw[:, k, :], xT[P * k:P * (k + 1), :]).then_inc(s_x[k], 16)
                if k == 4:
                    load_w(1)
            sp.dma_start(cst[:], consts).then_inc(s_cst, 16)
            for s in range(2, NS):
                load_w(s)
            sp.wait_ge(acc_done, ALL_GROUPS)
            sp.wait_ge(m_done, 2 * KS)
            for t in range(NT):
                sp.dma_start(hres[t][:], xtok[rows(t), :]).then_inc(s_res[t], 16)
            sp.wait_ge(m_hi, KS)
            sp.wait_ge(m_lo, KS)
            sp.dma_start(fnw[:], fnorm).then_inc(s_fn, 16)
            for t in range(NT):
                sp.wait_ge(h_out, t + 1)
                sp.dma_start(out[rows(t), :], hres[t][:]).then_inc(stored, 16)
            sp.wait_ge(stored, 16 * NT)

        @block.tensor
        def _(pe):
            def gemm(s, n0=0, n1=2 * MM):
                for n in range(n0, n1):
                    half, m = divmod(n, MM)
                    k, term = divmod(m, 3)
                    g = first_group(s) + half
                    if n == 0:
                        pe.wait_ge(w_hi, s + 1)
                        pe.wait_ge(w_lo, s + 1)
                    if m == 0:
                        pe.wait_ge(acc_out[g % 2], g // 2)
                    w = wlo if term == 2 else whi
                    x = xlo if term == 1 else xhi
                    mm = nc.tensor.matmul(B[g % 2][:], w[s % RING][:, k, :], x[:, k, HALF * half:HALF * (half + 1)],
                                          start=(m == 0), stop=(m == MM - 1))
                    if m == MM - 1:
                        mm.then_inc(acc_done, 1)

            def square_sums(src, banks):
                for i, b in enumerate(banks):
                    mm = nc.tensor.matmul(B[b][:], ones[:], src[:, i, :], start=True, stop=True)
                return mm

            pe.wait_ge(setup, 1)
            pe.wait_ge(w_hi, 1)
            pe.wait_ge(w_lo, 1)
            for k in range(KS):
                pe.wait_ge(x_hi, k + 1)
                pe.wait_ge(x_lo, k + 1)
                for half in range(2):
                    part = slice(HALF * half, HALF * (half + 1))
                    for term in range(3):
                        w = wlo if term == 2 else whi
                        x = xlo if term == 1 else xhi
                        mm = nc.tensor.matmul(B[half][:], w[0][:, k, :], x[:, k, part],
                                              start=(k == 0 and term == 0), stop=(k == KS - 1 and term == 2))
                    if k == KS - 1:
                        mm.then_inc(acc_done, 1)
                pe.wait_ge(x_sq, k + 1)
                for half in range(2):
                    part = slice(HALF * half, HALF * (half + 1))
                    nc.tensor.matmul(B[2 + half][:], ones[:], sqx[k % 2][:, part],
                                     start=(k == 0), stop=(k == KS - 1)).then_inc(ss_done, 1)
            for s in range(S_QKV, S_HQF):
                for half in range(2):
                    gemm(s, MM * half, MM * (half + 1))
                if s == 4:
                    pe.wait_ge(gb_row, 2)
                    pe.wait_ge(s_cst, 16)
                    for t in range(NT):
                        mm = nc.tensor.transpose(B[4][:, 64 * t:64 * (t + 1)], gb[:, P * t:P * (t + 1)],
                                                 ident[0:64, 0:64])
                    mm.then_inc(gb_turned, 1)
            leave(pe)

            for t in range(NT):
                fed = [0]

                def fill(n):
                    n = min(n, 2 * MM - fed[0])
                    gemm(S_HQF + t, fed[0], fed[0] + n)
                    fed[0] += n

                if t == 0:
                    fill(6)
                pe.wait_ge(sq_done, t + 1)
                square_sums(sq, [2, 3]).then_inc(ssq_done, 1)
                fill(3)
                if t:
                    pe.wait_ge(oa_out, t)
                    pe.wait_ge(s_ready, t + 1)
                else:
                    pe.wait_ge(gb_turned, 2)
                nc.tensor.matmul(B[4][:, 0:H], tri, gb_col[:, t, 0:H], start=True, stop=True)
                for h in range(H):
                    mm = nc.tensor.matmul(B[5][:, P * h:P * (h + 1)],
                                          gb_col[:, t, h:h + 1].broadcast_to([P, P]), tri, start=True, stop=True)
                mm.then_inc(gcum_done, 1)
                fill(3)
                pe.wait_ge(qk_norm, t + 1)
                for i, b in ((1, 2), (2, 3)):
                    for h in range(H):
                        mm = nc.tensor.transpose(B[b][:, P * h:P * (h + 1)], qkv(t)[:, H * i + h, :], ident)
                mm.then_inc(kv_turned, 1)
                for h in range(H):
                    pair = X[:, t + 1, 0:2 * HALF].rearrange("p (g h n) -> p g h n", g=2, h=H)[:, :, h, :]
                    mm = nc.tensor.matmul(B[6 + h // 2][:, 256 * (h % 2):256 * (h % 2 + 1)],
                                          qkv(t)[:, H + h, :], pair, start=True, stop=True)
                mm.then_inc(att_done, 1)
                fill(3)
                for lv in range(LV):
                    s = 1 << lv
                    if lv == 0:
                        pe.wait_ge(a_ready, t + 1)
                    else:
                        pe.wait_ge(t_ready, (LV * t + lv))
                    for h in range(H):
                        mm = nc.tensor.matmul(packed(B[6][:, 64 * h:64 * (h + 1)], s), AT[:, h, :],
                                              blocks(T[:, h:h + 1, :], s)[:, :, 0, :], start=True, stop=True)
                    mm.then_inc(u_psum, 1)
                    fill(3)
                    pe.wait_ge(u_ready, LV * t + lv + 1)
                    for h in range(H):
                        if lv < LV - 1:
                            nc.tensor.matmul(packed(B[7][:, 64 * h:64 * (h + 1)], s), TT[:, h, :],
                                             blocks(U[lv][:, h:h + 1, :], s)[:, :, 0, :], start=True, stop=True)
                    for h in range(H):
                        mm = nc.tensor.matmul(packed(B[7][:, 256 + 64 * h:256 + 64 * (h + 1)], s), U[lv][:, h, :],
                                              blocks(TT[:, h:h + 1, :], s)[:, :, 1, :], start=True, stop=True)
                    mm.then_inc(t_psum, 1)
                    fill(2 if lv < 6 else 0)
                pe.wait_ge(kg_done, 2 * (t + 1))
                pe.wait_ge(kd_ready, t + 1)
                pe.wait_ge(s_ready, t + 1)
                for h in range(H):
                    mm = nc.tensor.matmul(B[2][:, P * h:P * (h + 1)], kgT[:, P * h:P * (h + 1)], S[:, h, :],
                                          start=True, stop=True)
                mm.then_inc(ks_done, 1)
                fill(2)
                pe.wait_ge(x0_done, t + 1)
                pe.wait_ge(t_ready, LV * (t + 1))
                for h in range(H):
                    mm = nc.tensor.matmul(B[3][:, P * h:P * (h + 1)], TT[:, h, :], X0[:, P * h:P * (h + 1)],
                                          start=True, stop=True)
                mm.then_inc(tx_done, 1)
                fill(2)
                pe.wait_ge(vn_done, t + 1)
                for h in range(H):
                    nc.tensor.matmul(B[4][:, P * h:P * (h + 1)], S[:, h, :], qgT[:, P * h:P * (h + 1)],
                                     start=True, stop=False)
                    mm = nc.tensor.matmul(B[4][:, P * h:P * (h + 1)], vnew[:, h, :], QK[:, h, :],
                                          start=False, stop=True)
                mm.then_inc(o_done, 1)
                for h in range(H):
                    mm = nc.tensor.matmul(B[5][:, P * h:P * (h + 1)], kdec[:, h, :], vnew[:, h, :],
                                          start=True, stop=True)
                mm.then_inc(su_done, 1)
                fill(2 * MM)
            leave(pe)

            for u in range(NT):
                gemm(S_HI + u // 2, MM * (u % 2), MM * (u % 2) + 12)
                pe.wait_ge(o_sq, u + 1)
                if u:
                    pe.wait_ge(o_nrm, u)
                nc.tensor.matmul(B[3][:], ones[:], nrm[:], start=True, stop=True).then_inc(o_ss, 1)
                gemm(S_HI + u // 2, MM * (u % 2) + 12, MM * (u % 2) + 24)
                if u >= 1:
                    turn_hi = u - 1
                    out_of_bank(pe, 2 * S_HI + turn_hi)
                    if turn_hi:
                        pe.wait_ge(hi_out, turn_hi)
                    for i in range(4):
                        mm = nc.tensor.transpose(B[2][:, P * i:P * (i + 1)], hst[turn_hi % 2][:, P * i:P * (i + 1)],
                                                 ident)
                    mm.then_inc(hi_turned, 1)
            gemm(S_ZA, 0, 12)
            out_of_bank(pe, 2 * S_HI + NT - 1)
            pe.wait_ge(hi_out, NT - 1)
            for i in range(4):
                mm = nc.tensor.transpose(B[2][:, P * i:P * (i + 1)], hst[(NT - 1) % 2][:, P * i:P * (i + 1)], ident)
            mm.then_inc(hi_turned, 1)
            leave(pe)

            for t in range(NT):
                fed = [MM * (t % 2) + (12 if t == 0 else 0)]

                def fill(n):
                    n = min(n, MM * (t % 2 + 1) - fed[0])
                    gemm(S_ZA + t // 2, fed[0], fed[0] + n)
                    fed[0] += n

                pe.wait_ge(hk_lb, t + 1)
                for h in range(H):
                    mm = nc.tensor.matmul(B[4][:, P * h:P * (h + 1)], KR[:, h, :], X[:, h, P * t:P * (t + 1)],
                                          start=True, stop=True)
                mm.then_inc(hl_psum, 1)
                fill(2)
                for lv in range(LV):
                    s = 1 << lv
                    if lv == 0:
                        pe.wait_ge(qf_done, t + 1)
                    else:
                        pe.wait_ge(hl_upd, 2 * (LV * t + lv))
                    if lv >= 2:
                        pe.wait_ge(ha_done, (LV + 1) * t + lv)
                    for h in range(H):
                        mm = nc.tensor.matmul(packed(B[2 + lv % 2][:, 64 * h:64 * (h + 1)], s), KR[:, h, :],
                                              blocks(QP[:, h:h + 1, :], s)[:, :, 1, :], start=True, stop=True)
                    mm.then_inc(hl_psum, 1)
                    fill(3)
                pe.wait_ge(hl_upd, 2 * LV * (t + 1))
                for h in range(H):
                    mm = nc.tensor.transpose(B[5][:, P * h:P * (h + 1)], KR[:, h, :], ident)
                mm.then_inc(hk_turned, 1)
                fill(2)
                pe.wait_ge(ha_done, (LV + 1) * (t + 1))
                pe.wait_ge(hs_ready, t + 1)
                if t:
                    pe.wait_ge(ob_out, t)
                for h in range(H):
                    nc.tensor.matmul(B[6][:, P * h:P * (h + 1)], HS[:, h, :], QP[:, h, :], start=True, stop=False)
                    mm = nc.tensor.matmul(B[6][:, P * h:P * (h + 1)], hitok[:, t, h, :], HA[:, h, :],
                                          start=False, stop=True)
                mm.then_inc(ho_done, 1)
                pe.wait_ge(hk_out, t + 1)
                for h in range(H):
                    mm = nc.tensor.matmul(B[7][:, P * h:P * (h + 1)], kdt[:, h, :], hitok[:, t, h, :],
                                          start=True, stop=True)
                mm.then_inc(hs_done, 1)
                fill(24)
            leave(pe)

            for u in range(NT):
                gemm(S_ZB + u // 2, MM * (u % 2), MM * (u % 2) + 12)
                pe.wait_ge(o_sq, NT + u + 1)
                pe.wait_ge(o_nrm, NT + u)
                nc.tensor.matmul(B[3][:], ones[:], nrm[:], start=True, stop=True).then_inc(o_ss, 1)
                gemm(S_ZB + u // 2, MM * (u % 2) + 12, MM * (u % 2) + 24)
            leave(pe)

            for d in range(KS):
                gemm(S_MERGE + 3 * d)
                gemm(S_MERGE + 3 * d + 1)
                s = S_MERGE + 3 * d + 2
                pe.wait_ge(w_hi, s + 1)
                pe.wait_ge(w_lo, s + 1)
                if d == 0:
                    pe.wait_ge(y_hi, 2 * H)
                    pe.wait_ge(y_lo, 2 * H)
                for half in range(2):
                    part = slice(HALF * half, HALF * (half + 1))
                    for br in range(2):
                        g = first_group(s) + 2 * half + br
                        pe.wait_ge(acc_out[g % 2], g // 2)
                        for h in range(H):
                            for term in range(3):
                                w = wlo if term == 2 else whi
                                y = ylo if term == 1 else yhi
                                mm = nc.tensor.matmul(B[g % 2][:], w[s % RING][:, H * br + h, :], y[br][:, h, part],
                                                      start=(h == 0 and term == 0),
                                                      stop=(h == H - 1 and term == 2))
                        mm.then_inc(acc_done, 1)

            def out_product(t, k, e, last):
                part = slice(HALF * e, HALF * (e + 1))
                for term in range(3):
                    m = xlo if term == 1 else xhi
                    w = wolo if term == 2 else wohi
                    mm = nc.tensor.matmul(B[t][:], m[:, k, P * t:P * (t + 1)], w[:, k, part],
                                          start=(k == 0 and term == 0), stop=(k == KS - 1 and term == 2))
                if last:
                    mm.then_inc(out_done, 1)

            pe.wait_ge(acc_out[0], ALL_GROUPS // 2)
            pe.wait_ge(acc_out[1], ALL_GROUPS // 2)
            for k in range(KS):
                pe.wait_ge(m_hi, k + 1)
                pe.wait_ge(m_lo, k + 1)
                pe.wait_ge(w_hi, S_OUT + k + 1)
                pe.wait_ge(w_lo, S_OUT + k + 1)
                for t in range(NT):
                    out_product(t, k, 0, k == KS - 1)
            for t in range(NT):
                pe.wait_ge(h_res, t + 1)
                for k in range(KS):
                    out_product(t, k, 1, k == KS - 1)

        def split_target(s):
            if s < S_OUT:
                return whi[s % RING][:], wlo[s % RING][:]
            k = s - S_OUT
            cut = "p (k n) -> p k n"
            return wohi[:, k, :].rearrange(cut, k=KS), wolo[:, k, :].rearrange(cut, k=KS)

        def split_waits(eng, s):
            eng.wait_ge(s_w[s % 2], 16 * (s // 2 + 1))
            if s >= S_OUT:
                eng.wait_ge(acc_done, ALL_GROUPS)
            elif s >= RING:
                eng.wait_ge(acc_done, end_group(s - RING))

        @block.scalar
        def _(act):
            def link(ins, n=[0]):
                n[0] += 1
                ins.then_inc(astep, 1)
                act.wait_ge(astep, n[0])

            def split_hi(s):
                split_waits(act, s)
                nc.scalar.activation(split_target(s)[0], wraw[s % 2][:], ACT.Identity).then_inc(w_hi, 1)

            nc.scalar.preload_act_table_set("natural_log_exp_and_others")
            act.wait_ge(setup, 1)
            act.wait_ge(s_prm, 16)
            split_hi(0)
            for k in range(KS):
                act.wait_ge(s_x[k], 16)
                nc.scalar.activation(xhi[:, k, :], xraw[:, k, :], ACT.Identity, scale=nw[:, k:k + 1]).then_inc(x_hi, 1)
                if k >= 2:
                    act.wait_ge(ss_done, 2 * (k - 1))
                nc.scalar.activation(sqx[k % 2][:], xraw[:, k, :], ACT.Square).then_inc(x_sq, 1)
            split_hi(1)
            act.wait_ge(ss_done, 2 * KS)
            for half in range(2):
                part = rms[:, HALF * half:HALF * (half + 1)]
                link(nc.scalar.activation(part, B[2 + half][:], ACT.Ln, bias=eps, scale=1.0 / DM))
                nc.scalar.activation(part, part, ACT.Exp, scale=-0.5).then_inc(rms_done, 1)
            nc.scalar.activation(nega, alog, ACT.Exp).then_inc(ab_act, 1)
            act.wait_ge(ab_row, 1)
            nc.scalar.activation(lbe, lbe, ACT.Exp).then_inc(ab_act, 1)
            act.wait_ge(ab_row, 2)
            link(nc.scalar.activation(ab2[:], ab2[:], ACT.Exp))
            nc.scalar.activation(ab2[:], ab2[:], ACT.Ln, bias=one[0:H]).then_inc(ab_act, 1)
            nc.scalar.activation(ab[32:32 + H, :], ab[32:32 + H, :], ACT.Exp, scale=-1.0).then_inc(ab_act, 1)
            split_hi(2)

            def silu(u):
                s, half = S_QKV + u // 2, u % 2
                act.wait_ge(conv_done, u + 1)
                c = s - S_QKV
                dst = X[:, 4 * half + 1:4 * half + 5, P * c:P * (c + 1)]
                nc.scalar.activation(dst, conv[half][:].rearrange("p (t n) -> p t n", n=P),
                                     ACT.Silu).then_inc(silu_done, 1)

            for u in range(2 * (S_HQF - S_QKV)):
                c, half = divmod(u, 2)
                out_of_bank(act, 2 * S_QKV + u)
                if u >= 2:
                    act.wait_ge(silu_done, u - 1)
                nc.scalar.activation(conv[half][:], pre[:, HALF * half:HALF * (half + 1)], ACT.Identity,
                                     scale=cw[:, c, 0:1]).then_inc(tap_done, 1)
                if u:
                    silu(u - 1)
                if half:
                    split_hi(S_QKV + c + 2)
            silu(2 * (S_HQF - S_QKV) - 1)
            leave(act)
            enter(act, 1)

            nc.scalar.preload_act_table_set("natural_log_exp_and_others")

            def squares(t):
                if t:
                    act.wait_ge(o_done, t)
                nc.scalar.activation(sq[:].rearrange("p g n -> p (g n)"), X[:, t + 1, 0:2 * HALF],
                                     ACT.Square).then_inc(sq_done, 1)

            for t in range(NT):
                squares(t)
                act.wait_ge(ssq_done, t + 1)
                for i in range(2):
                    link(nc.scalar.activation(sq[:, i, :], B[2 + i][:], ACT.Ln, bias=eps))
                    nc.scalar.activation(sq[:, i, :], sq[:, i, :], ACT.Exp, scale=-0.5).then_inc(rs_done, 1)
                act.wait_ge(dif_done, t + 1)
                nc.scalar.activation(dec[:], dec[:], ACT.Exp).then_inc(dec_done, 1)
                if t:
                    act.wait_ge(s_ready, t + 1)
                nc.scalar.activation(egr[:].rearrange("p h n -> p (h n)"), B[5][:], ACT.Exp).then_inc(egr_done, 1)
                nc.scalar.activation(kdc, gle, ACT.Exp).then_inc(kdc_done, 1)
                act.wait_ge(kv_turned, t + 1)
                nc.scalar.activation(vtok[:], B[3][:], ACT.Identity).then_inc(v_out, 1)
                split_hi(S_HQF + t + 2)
                act.wait_ge(o_done, t + 1)
                nc.scalar.activation(X[:, t, 2 * HALF:3 * HALF], B[4][:], ACT.Identity).then_inc(oa_out, 1)
            leave(act)
            enter(act, 2)

            def out_squares(u, src):
                if u:
                    act.wait_ge(o_nrm, u)
                nc.scalar.activation(nrm[:].rearrange("p (a b) -> p a b", b=P), src, ACT.Square).then_inc(o_sq, 1)
                act.wait_ge(o_ss, u + 1)
                link(nc.scalar.activation(nrm[:], B[3][:], ACT.Ln, bias=eps, scale=1.0 / P))
                nc.scalar.activation(nrm[:], nrm[:], ACT.Exp, scale=-0.5).then_inc(o_rs, 1)

            def hi_copy(u):
                act.wait_ge(hi_turned, u + 1)
                c, half = divmod(u, 2)
                nc.scalar.activation(hitok[:, 4 * half:4 * half + 4, c, :],
                                     B[2][:].rearrange("p (t n) -> p t n", n=P), ACT.Identity).then_inc(hi_out, 1)

            for u in range(NT):
                out_squares(u, X[:, u, 2 * HALF:3 * HALF].rearrange("p (a b) -> p a b", b=P))
                if u % 2:
                    split_hi(S_HI + u // 2 + 2)
                if u:
                    hi_copy(u - 1)
            hi_copy(NT - 1)
            leave(act)
            enter(act, 3)

            def z_gate(u):
                out_of_bank(act, 2 * S_ZA + u)
                nc.scalar.activation(sg[u % 2][:], zr[u % 2][:], ACT.Sigmoid).then_inc(z_sig, 1)

            for t in range(NT):
                tile = X[:, 4:8, P * t:P * (t + 1)]
                if t:
                    act.wait_ge(hs_ready, t + 1)
                nc.scalar.activation(FF[:], tile, ACT.Sigmoid).then_inc(hf_sig, 1)
                nc.scalar.activation(KR[:], tile, ACT.Sigmoid, scale=-1.0).then_inc(hf_sig, 1)
                if t % 2:
                    split_hi(S_ZA + t // 2 + 2)
                if t:
                    z_gate(t - 1)
                act.wait_ge(hk_turned, t + 1)
                nc.scalar.activation(kdt[:].rearrange("p h n -> p (h n)"), B[5][:], ACT.Identity).then_inc(hk_out, 1)
                act.wait_ge(ho_done, t + 1)
                nc.scalar.activation(X[:, 0:4, P * t:P * (t + 1)], B[6][:].rearrange("p (h n) -> p h n", n=P),
                                     ACT.Identity).then_inc(ob_out, 1)

            z_gate(NT - 1)
            leave(act)
            enter(act, 4)

            for u in range(NT):
                nc.scalar.preload_act_table_set("natural_log_exp_and_others")
                out_squares(NT + u, X[:, u // 2, HALF * (u % 2):HALF * (u % 2 + 1)].rearrange("p (a b) -> p a b", b=P))
                if u % 2:
                    split_hi(S_ZB + u // 2 + 2)
                z_gate(NT + u)
            leave(act)
            enter(act, 5)

            for h in range(H):
                nc.scalar.activation(yhi[0][:, h, :].rearrange("p (t n) -> p t n", n=P),
                                     X[:, 0:NT, 2 * HALF + P * h:2 * HALF + P * (h + 1)], ACT.Identity).then_inc(y_hi, 1)
            act.wait_ge(y_lo, H)
            for h in range(H):
                nc.scalar.activation(yhi[1][:, h, :], X[:, h, 0:TOK], ACT.Identity).then_inc(y_hi, 1)
            for d in range(KS):
                for r in range(2):
                    for half in range(2):
                        out_of_bank(act, first_group(S_MERGE + 3 * d + r) + half)
                        buf = (gateb if r else merged[d])[:, HALF * half:HALF * (half + 1)]
                        nc.scalar.activation(buf, buf, ACT.Sigmoid).then_inc(g_sig, 1)
                    if d < KS - 1 or r == 0:
                        split_hi(S_MERGE + 3 * d + r + 2)
                if d < KS - 1:
                    split_hi(S_MERGE + 3 * d + 4)
            act.wait_ge(acc_done, first_group(S_OUT - 1))
            for k in range(KS):
                act.wait_ge(m_done, 2 * (k + 1))
                nc.scalar.activation(xhi[:, k, :], merged[k][:], ACT.Identity).then_inc(m_hi, 1)
                if k == KS - 2:
                    split_hi(S_OUT)
            for k in range(1, KS):
                split_hi(S_OUT + k)
            nc.scalar.preload_act_table_set("natural_log_exp_and_others")
            for t in range(NT):
                act.wait_ge(h_res, NT + t + 1)
                link(nc.scalar.activation(scr[:], hres[t][:], ACT.Square, accum_out=ssh[:, t, 0:1]))
                link(nc.scalar.activation(rh[:, t:t + 1], ssh[:, t, 0:1], ACT.Ln, bias=eps, scale=1.0 / DM))
                nc.scalar.activation(rh[:, t:t + 1], rh[:, t:t + 1], ACT.Exp, scale=-0.5).then_inc(h_rs, 1)

        @block.gpsimd
        def _(pool):
            def split_lo(s):
                split_waits(pool, s)
                pool.wait_ge(w_hi, s + 1)
                hi, lo = split_target(s)
                nc.gpsimd.tensor_tensor(lo, wraw[s % 2][:], hi.bitcast(F32), ALU.subtract).then_inc(w_lo, 1)

            nc.gpsimd.memset(ones[:], 1.0)
            nc.gpsimd.memset(one, 1.0)
            nc.gpsimd.memset(eps, EPS).then_inc(setup, 1)
            for s in range(S_HQF + 2):
                split_lo(s)
            leave(pool)
            enter(pool, 1)
            for i in range(LV):
                nc.gpsimd.memset(U[i][:], 0.0)
            nc.gpsimd.memset(S[:], 0.0).then_inc(s_ready, 1)
            for t in range(NT):
                pool.wait_ge(dec_done, t + 1)
                nc.gpsimd.tensor_tensor(decm[:], dec[:], tri[:, None, :].broadcast_to([P, H, P]),
                                        ALU.mult).then_inc(decm_done, 1)
                pool.wait_ge(egr_done, t + 1)
                pool.wait_ge(qk_norm, t + 1)
                for i, dst in ((1, kgT), (0, qgT)):
                    nc.gpsimd.tensor_tensor(dst, X[:, t + 1, HALF * i:HALF * (i + 1)],
                                            egr[:].rearrange("p h n -> p (h n)"), ALU.mult).then_inc(kg_done, 1)
                split_lo(S_HQF + t + 2)
            leave(pool)
            enter(pool, 2)
            for u in range(NT):
                if u % 2:
                    split_lo(S_HI + u // 2 + 2)
            leave(pool)
            enter(pool, 3)
            nc.gpsimd.memset(HS[:], 0.0).then_inc(hs_ready, 1)

            def z_apply(u):
                c, half = divmod(u % NT, 2)
                if u < NT:
                    o = X[:, 4 * half:4 * half + 4, 2 * HALF + P * c:2 * HALF + P * (c + 1)]
                else:
                    o = X[:, c, HALF * half:HALF * (half + 1)].rearrange("p (a b) -> p a b", b=P)
                pool.wait_ge(z_sig, u + 1)
                z3 = zr[u % 2][:].rearrange("p (a b) -> p a b", b=P)
                nc.gpsimd.tensor_tensor(z3, z3, sg[u % 2][:].rearrange("p (a b) -> p a b", b=P),
                                        ALU.mult).then_inc(pstep, 1)
                pool.wait_ge(pstep, u + 1)
                if u >= NT:
                    pool.wait_ge(o_nrm, u + 1)
                nc.gpsimd.tensor_tensor(o, o, z3, ALU.mult).then_inc(z_y, 1)

            for t in range(NT):
                pool.wait_ge(hf_sig, 2 * (t + 1))
                nc.gpsimd.tensor_tensor(KR[:], KR[:], by_head(omlb), ALU.mult).then_inc(hk_lb, 1)
                for lv in range(LV):
                    s = 1 << lv
                    pool.wait_ge(hl_psum, (LV + 1) * t + lv + 2)
                    if lv == 0:
                        pool.wait_ge(hf_f, t + 1)
                    else:
                        pool.wait_ge(hl_upd, 2 * (LV * t + lv))
                    k_even = blocks(KR[:], s)[:, :, 0, :]
                    nc.gpsimd.tensor_tensor(k_even, k_even, totals(lv)[:, :, 1:2].broadcast_to([P, H * 64 // s, s]),
                                            ALU.mult).then_inc(hl_upd, 1)
                if t % 2:
                    split_lo(S_ZA + t // 2 + 2)
                if t:
                    z_apply(t - 1)
            z_apply(NT - 1)
            leave(pool)
            enter(pool, 4)
            for u in range(NT):
                if u % 2:
                    split_lo(S_ZB + u // 2 + 2)
                z_apply(NT + u)
            leave(pool)
            enter(pool, 5)
            for s in range(S_MERGE + 2, NS):
                split_lo(s)

        @block.vector
        def _(dve):
            V = nc.vector
            steps = [0]

            def link(ins):
                steps[0] += 1
                ins.then_inc(dstep, 1)
                dve.wait_ge(dstep, steps[0])

            def take(g, dst, rows_=P):
                dve.wait_ge(acc_done, g + 1)
                half = g % 2
                r = rms[0:rows_, HALF * half:HALF * (half + 1)]
                b = B[half][0:rows_, :]
                if len(dst.shape) == 3:
                    r, b = (a.rearrange("p (t n) -> p t n", n=P) for a in (r, b))
                V.tensor_tensor(dst, b, r, ALU.mult).then_inc(acc_out[half], 1)

            dve.wait_ge(s_prm, 16)
            V.memset(pre[:, 0:3], 0.0)
            link(V.memset(gb[:], 0.0))
            V.tensor_tensor(lbe, lbl, lbl, ALU.subtract).then_inc(ab_row, 1)
            for k in range(KS):
                dve.wait_ge(x_hi, k + 1)
                V.scalar_tensor_tensor(out=xlo[:, k, :], in0=xraw[:, k, :], scalar=nw[:, k:k + 1],
                                       in1=xhi[:, k, :].bitcast(F32), op0=ALU.mult,
                                       op1=ALU.subtract).then_inc(x_lo, 1)
            dve.wait_ge(rms_done, 2)
            take(0, ab[:, 0:HALF], 64)
            take(1, ab[:, HALF:TOK], 64)

            def decays(n):
                if n == 0:
                    dve.wait_ge(acc_out[0], 1)
                    dve.wait_ge(acc_out[1], 1)
                    V.tensor_scalar(ab1[:], ab[0:H, :], dtb, 0.0, ALU.add, ALU.max)
                    link(V.tensor_scalar(ab2[:], ab[0:H, :], dtb, None, ALU.add))
                    link(V.tensor_scalar(gb[0:H, :], ab2[:], -1.0, None, ALU.mult))
                    V.tensor_tensor(ab2[:], ab2[:], gb[0:H, :], ALU.min).then_inc(ab_row, 1)
                elif n == 1:
                    dve.wait_ge(ab_act, 1)
                    link(V.tensor_scalar(nega, nega, -1.0, None, ALU.mult))
                    dve.wait_ge(ab_act, 3)
                    link(V.tensor_tensor(ab1[:], ab1[:], ab2[:], ALU.add))
                    V.tensor_scalar(gb[0:H, :], ab1[:], nega, None, ALU.mult).then_inc(gb_row, 1)
                elif n == 2:
                    dve.wait_ge(ab_act, 4)
                    link(V.tensor_scalar(ab[32:32 + H, :], ab[32:32 + H, :], 1.0, None, ALU.add))
                    V.reciprocal(gb[32:32 + H, :], ab[32:32 + H, :]).then_inc(gb_row, 1)
                elif n == 3:
                    link(V.reciprocal(lb, lbe))
                    link(V.tensor_tensor(lbe, lbe, lb, ALU.mult))
                    link(V.tensor_tensor(lb, lbe, lbe, ALU.subtract))
                    V.tensor_scalar(omlb, lb, -1.0, 1.0, ALU.mult, ALU.add)
                elif n == 8:
                    dve.wait_ge(gb_turned, 1)
                    V.tensor_copy(gb_col[:].rearrange("p t n -> p (t n)"), B[4][:]).then_inc(gb_turned, 1)

            decays(0)
            for u in range(2 * (S_HQF - S_QKV)):
                c, half = divmod(u, 2)
                if u:
                    dve.wait_ge(conv_done, u)
                take(2 * S_QKV + u, pre[:, 3 + HALF * half:3 + HALF * (half + 1)])
                dve.wait_ge(tap_done, u + 1)
                for j in range(1, 4):
                    ins = V.scalar_tensor_tensor(out=conv[half][:], in0=pre[:, HALF * half + j:HALF * (half + 1) + j],
                                                 scalar=cw[:, c, j:j + 1], in1=conv[half][:], op0=ALU.mult,
                                                 op1=ALU.add)
                    if j < 3:
                        link(ins)
                ins.then_inc(conv_done, 1)
                if u:
                    decays(u)
            leave(dve)
            enter(dve, 1)

            for t in range(NT):
                dve.wait_ge(rs_done, 2 * (t + 1))
                q, k = X[:, t + 1, 0:HALF], X[:, t + 1, HALF:2 * HALF]
                V.scalar_tensor_tensor(out=q, in0=q, scalar=QSCALE, in1=sq[:, 0, :], op0=ALU.mult, op1=ALU.mult)
                V.tensor_tensor(k, k, sq[:, 1, :], ALU.mult).then_inc(qk_norm, 1)
                dve.wait_ge(gcum_done, t + 1)
                link(V.tensor_copy(gcs, B[4][:, 0:H]))
                for h in range(H):
                    V.tensor_scalar(dec[:, h, :], B[5][:, P * h:P * (h + 1)], gcs[:, h:h + 1], 0.0,
                                    ALU.subtract, ALU.min)
                V.tensor_tensor(gle, B[5][:].rearrange("p (h n) -> p h n", n=P)[:, :, P - 1], gcs,
                                ALU.subtract).then_inc(dif_done, 1)
                for m in (T, TT):
                    V.tensor_copy(m[:], ident[:, None, :].broadcast_to([P, H, P]))
                dve.wait_ge(kv_turned, t + 1)
                dve.wait_ge(kdc_done, t + 1)
                V.tensor_tensor(kdec[:], B[2][:].rearrange("p (h n) -> p h n", n=P), by_head(kdc),
                                ALU.mult).then_inc(kd_ready, 1)
                dve.wait_ge(att_done, t + 1)
                dve.wait_ge(dec_done, t + 1)
                for h in range(H):
                    V.scalar_tensor_tensor(out=AT[:, h, :],
                                           in0=B[6 + h // 2][:, 256 * (h % 2) + P:256 * (h % 2) + 2 * P],
                                           scalar=gb_col[:, t, 32 + h:33 + h], in1=dec[:, h, :], op0=ALU.mult,
                                           op1=ALU.mult)
                dve.wait_ge(decm_done, t + 1)
                for i in range(2):
                    ins = V.tensor_tensor(QK[:, 2 * i:2 * i + 2, :],
                                          B[6 + i][:].rearrange("p (h n) -> p h n", n=2 * P)[:, :, 0:P],
                                          decm[:, 2 * i:2 * i + 2, :], ALU.mult)
                ins.then_inc(a_ready, 1)
                for lv in range(LV):
                    s = 1 << lv
                    cut = "p h (b e s) -> p h b e s"
                    dve.wait_ge(u_psum, LV * t + lv + 1)
                    V.tensor_tensor(U[lv][:].rearrange(cut, e=2, s=s)[:, :, :, 0, :],
                                    B[6][:, 0:256].rearrange("p (h b s) -> p h b s", h=H, s=s),
                                    mask(inv_mask, lv), ALU.mult).then_inc(u_ready, 1)
                    dve.wait_ge(t_psum, LV * t + lv + 1)
                    if lv < LV - 1:
                        even = blocks(T[:], s)[:, :, 0, :]
                        V.tensor_tensor(even, packed(B[7][:, 0:256], s), even, ALU.add)
                    odd = blocks(TT[:], s)[:, :, 1, :]
                    V.tensor_tensor(odd, packed(B[7][:, 256:512], s), odd, ALU.add).then_inc(t_ready, 1)
                    if lv == 5:
                        take(2 * (S_HQF + t), X[:, t, 0:HALF])
                dve.wait_ge(ks_done, t + 1)
                dve.wait_ge(v_out, t + 1)
                V.tensor_tensor(X0[:], vtok[:], B[2][:], ALU.subtract).then_inc(x0_done, 1)
                dve.wait_ge(tx_done, t + 1)
                V.tensor_tensor(vnew[:], B[3][:].rearrange("p (h n) -> p h n", n=P), by_head(gb_col[:, t, 32:32 + H]),
                                ALU.mult).then_inc(vn_done, 1)
                dve.wait_ge(su_done, t + 1)
                for h in range(H):
                    ins = V.scalar_tensor_tensor(out=S[:, h, :], in0=S[:, h, :], scalar=egr[:, h, P - 1:P],
                                                 in1=B[5][:, P * h:P * (h + 1)], op0=ALU.mult, op1=ALU.add)
                ins.then_inc(s_ready, 1)
                take(2 * (S_HQF + t) + 1, X[:, t, HALF:TOK])
            leave(dve)
            enter(dve, 2)

            for u in range(NT):
                if u >= 2:
                    dve.wait_ge(hi_turned, u - 1)
                take(2 * S_HI + u, hst[u % 2][:])
                dve.wait_ge(o_rs, u + 1)
                o = X[:, u, 2 * HALF:3 * HALF]
                V.scalar_tensor_tensor(out=o, in0=o, scalar=gnw, in1=nrm[:], op0=ALU.mult,
                                       op1=ALU.mult).then_inc(o_nrm, 1)
            leave(dve)
            enter(dve, 3)

            def take_z(u):
                if u >= 2:
                    dve.wait_ge(z_y, u - 1)
                take(2 * S_ZA + u, zr[u % 2][:])

            for t in range(NT):
                dve.wait_ge(hf_sig, 2 * (t + 1))
                link(V.tensor_tensor(FF[:], FF[:], by_head(omlb), ALU.mult))
                steps[0] += 0
                V.tensor_tensor(FF[:], FF[:], by_head(lb), ALU.add).then_inc(hf_f, 1)
                dve.wait_ge(hf_f, t + 1)
                V.tensor_tensor(QP[:], X[:, 0:H, P * t:P * (t + 1)], FF[:], ALU.mult).then_inc(qf_done, 1)
                dve.wait_ge(hl_psum, (LV + 1) * t + 1)
                V.tensor_tensor(HA[:], B[4][:].rearrange("p (h n) -> p h n", n=P),
                                ident[:, None, :].broadcast_to([P, H, P]), ALU.mult).then_inc(ha_done, 1)
                if t:
                    take_z(t - 1)
                for lv in range(LV):
                    s = 1 << lv
                    cut = "p h (b e s) -> p h b e s"
                    tot = totals(lv)
                    dst = totals(lv + 1)
                    if lv < LV - 1:
                        dst = dst.rearrange("p b e -> p (b e)")
                    else:
                        dst = TOT[:, 504:508]
                    V.tensor_tensor(dst, tot[:, :, 0], tot[:, :, 1], ALU.mult).then_inc(dstep, 1)
                    steps[0] += 1
                    dve.wait_ge(hl_psum, (LV + 1) * t + lv + 2)
                    q_odd = blocks(QP[:], s)[:, :, 1, :]
                    V.tensor_tensor(q_odd, q_odd, tot[:, :, 0:1].broadcast_to([P, H * 64 // s, s]),
                                    ALU.mult).then_inc(hl_upd, 1)
                    dve.wait_ge(ha_done, (LV + 1) * t + lv + 1)
                    V.copy_predicated(HA[:].rearrange(cut, e=2, s=s)[:, :, :, 1, :], mask(hg_mask.bitcast(I32), lv),
                                      B[2 + lv % 2][:, 0:256].rearrange("p (h b s) -> p h b s", h=H, s=s)
                                      ).then_inc(ha_done, 1)
                    dve.wait_ge(dstep, steps[0])
                dve.wait_ge(hs_done, t + 1)
                for h in range(H):
                    ins = V.scalar_tensor_tensor(out=HS[:, h, :], in0=HS[:, h, :], scalar=TOT[:, 504 + h:505 + h],
                                                 in1=B[7][:, P * h:P * (h + 1)], op0=ALU.mult, op1=ALU.add)
                ins.then_inc(hs_ready, 1)
            take_z(NT - 1)
            leave(dve)
            enter(dve, 4)

            for u in range(NT):
                take_z(NT + u)
                dve.wait_ge(o_rs, NT + u + 1)
                o = X[:, u // 2, HALF * (u % 2):HALF * (u % 2 + 1)]
                V.scalar_tensor_tensor(out=o, in0=o, scalar=hnw, in1=nrm[:], op0=ALU.mult,
                                       op1=ALU.mult).then_inc(o_nrm, 1)
            leave(dve)
            enter(dve, 5)

            def split_y(br, h):
                dve.wait_ge(y_hi, H * br + h + 1)
                if br:
                    y, cut = X[:, h, 0:TOK], "p n -> p n"
                    hi, lo = yhi[br][:, h, :], ylo[br][:, h, :]
                else:
                    y = X[:, 0:NT, 2 * HALF + P * h:2 * HALF + P * (h + 1)]
                    hi, lo = (a[:, h, :].rearrange("p (t n) -> p t n", n=P) for a in (yhi[br], ylo[br]))
                V.tensor_tensor(lo, y, hi.bitcast(F32), ALU.subtract).then_inc(y_lo, 1)

            def take_gate(d, r, half):
                take(first_group(S_MERGE + 3 * d + r) + half,
                     (gateb if r else merged[d])[:, HALF * half:HALF * (half + 1)])

            for h in range(H):
                split_y(0, h)
            take_gate(0, 0, 0)
            for h in range(2):
                split_y(1, h)
            take_gate(0, 0, 1)
            for h in range(2, H):
                split_y(1, h)
            for d in range(KS):
                for r in range(2):
                    for half in range(2):
                        if d:
                            dve.wait_ge(m_done, 2 * d)
                        if d or r:
                            take_gate(d, r, half)
                if d == KS - 1:
                    dve.wait_ge(acc_done, first_group(S_OUT - 1))
                    for k in range(KS - 1):
                        dve.wait_ge(m_hi, k + 1)
                        V.tensor_tensor(xlo[:, k, :], merged[k][:], xhi[:, k, :].bitcast(F32),
                                        ALU.subtract).then_inc(m_lo, 1)
                for half in range(2):
                    part = slice(HALF * half, HALF * (half + 1))
                    dve.wait_ge(g_sig, 4 * (d + 1))
                    for br, gate in ((0, merged[d]), (1, gateb)):
                        g = first_group(S_MERGE + 3 * d + 2) + 2 * half + br
                        dve.wait_ge(acc_done, g + 1)
                        V.tensor_tensor(gate[:, part], B[g % 2][:], gate[:, part], ALU.mult).then_inc(acc_out[g % 2], 1)
                        out_of_bank(dve, g)
                    V.tensor_tensor(merged[d][:, part], merged[d][:, part], gateb[:, part],
                                    ALU.add).then_inc(m_done, 1)
            dve.wait_ge(m_hi, KS)
            V.tensor_tensor(xlo[:, KS - 1, :], merged[KS - 1][:], xhi[:, KS - 1, :].bitcast(F32),
                            ALU.subtract).then_inc(m_lo, 1)
            for e in range(2):
                for t in range(NT):
                    if e == 0:
                        dve.wait_ge(s_res[t], 16)
                    dve.wait_ge(out_done, NT * e + t + 1)
                    part = hres[t][:, HALF * e:HALF * (e + 1)]
                    V.tensor_tensor(part, B[t][:], part, ALU.add).then_inc(h_res, 1)
                    if e:
                        if t == 0:
                            dve.wait_ge(s_fn, 16)
                        dve.wait_ge(h_rs, t + 1)
                        V.scalar_tensor_tensor(out=hres[t][:], in0=hres[t][:], scalar=rh[:, t:t + 1], in1=fnw[:],
                                               op0=ALU.mult, op1=ALU.mult).then_inc(h_out, 1)


def level_masks():
    import numpy as np
    inv = np.zeros((P, LV, 64), np.float32)
    hg = np.zeros((P, LV, 64), np.float32)
    for lv in range(LV):
        s = 1 << lv
        for c in range(64):
            first = c // s * 2 * s
            inv[first + s:first + 2 * s, lv, c] = -1.0
            hg[first:first + s, lv, c] = 1.0
    return inv.reshape(P, -1), hg.reshape(P, -1)


def kernel(**inputs):
    import numpy as np
    import concourse.bacc as bacc
    from concourse.bass_utils import run_bass_kernel_spmd

    a = {k: np.asarray(v) for k, v in inputs.items()}
    f = np.float32
    x = np.ascontiguousarray(a["x"][0])
    w_in = a["w_in"][0]
    qk, v, heads, wide = H * P, H * P, H, H * P
    cuts = np.cumsum([2 * qk + v, heads, heads, v, wide, wide, wide, wide])
    c_qkv, c_a, c_b, c_za, c_hq, c_hf, c_hi, c_zb, c_gate = np.split(w_in, cuts, axis=1)
    w_ab = np.zeros((DM, P), f)
    w_ab[:, 0:H], w_ab[:, 32:32 + H] = c_a, c_b
    gate_a, gate_b = np.split(c_gate, 2, axis=1)

    def tiles(w):
        return list(w.reshape(w.shape[0] // P, P, w.shape[1] // P, P).transpose(2, 1, 0, 3))

    order = [*tiles(w_ab), *tiles(c_qkv), *tiles(c_hq), *tiles(c_hf), *tiles(c_hi), *tiles(c_za), *tiles(c_zb)]
    branches = a["w_branch"][0].reshape(2 * H * P, DM)
    for g0, g1, br in zip(tiles(gate_a), tiles(gate_b), tiles(branches)):
        order += [g0, g1, br]
    order += list(a["w_out"][0].reshape(KS, P, KS, P))
    w_tiles = np.ascontiguousarray(np.stack(order)).reshape(NS, P, KS * P)

    params = np.zeros((P, 64), f)
    params[:, 0:KS] = a["norm_w"][0].reshape(KS, P).T
    params[:, 8:56] = a["conv_w"][0].reshape(4, 12, P).transpose(2, 1, 0).reshape(P, 48)
    params[:, 56], params[:, 57] = a["gdn_norm_w"][0], a["hg_norm_w"][0]
    params[:, 58:62] = a["hg_lb_logits"][0].reshape(H, P).T
    params[0:H, 62], params[0:H, 63] = a["a_log"][0], a["dt_bias"][0]
    consts = np.concatenate([np.eye(P, dtype=f), np.triu(np.ones((P, P), f)), *level_masks()], axis=1)

    nc = bacc.Bacc("TRN2", target_bir_lowering=False, num_devices=1)
    arrays = {"xT": np.ascontiguousarray(x.T), "xtok": x, "w_tiles": w_tiles, "params": params,
              "fnorm": np.ascontiguousarray(np.broadcast_to(a["final_norm_w"], (P, DM))), "consts": consts}
    aps = [nc.dram_tensor(n, v.shape, mybir.dt.from_np(v.dtype), kind="ExternalInput").ap()
           for n, v in arrays.items()]
    out = nc.dram_tensor("out", (TOK, DM), F32, kind="ExternalOutput").ap()
    bass_hybrid_gdn_hgrn2(nc, *aps, out)
    r = run_bass_kernel_spmd(nc, [arrays], core_ids=[0])
    return r.results[0]["out"].reshape(1, TOK, DM)
```

```python
from contextlib import ExitStack

import concourse.bass as bass
from concourse import mybir

F32 = mybir.dt.float32
F32R = mybir.dt.float32r
I32 = mybir.dt.int32
ALU = mybir.AluOpType
ACT = mybir.ActivationFunctionType

P = 128
TOK = 1024
DM = 1024
NT = TOK // P
KS = DM // P
H = 4
HALF = 512
EPS = 1e-6
LV = 7
QSCALE = float(P) ** -0.5
MM = 3 * KS

S_AB, S_QKV, S_HQF, S_HI, S_ZA, S_ZB, S_MERGE = 0, 1, 13, 21, 25, 29, 33
S_OUT = S_MERGE + 3 * KS
NS = S_OUT + KS
RING = 3


def first_group(s):
    if s < S_MERGE:
        return 2 * s
    d, r = divmod(s - S_MERGE, 3)
    return 2 * S_MERGE + 8 * d + 2 * r


def end_group(s):
    return first_group(s + 1)


ALL_GROUPS = first_group(S_OUT)


def bass_hybrid_gdn_hgrn2(nc, xT, xtok, w_tiles, params, fnorm, consts, out):
    with ExitStack() as ctx:
        def place(name, shape, dt, offset):
            return nc.alloc_sbuf_tensor_at(name, shape, dt, offset=offset)

        def stack(top):
            def sb(name, shape, dt=F32):
                size = 4
                for n in shape[1:]:
                    size *= n
                t = place(name, shape, dt, top[0])
                top[0] += (size + 31) // 32 * 32
                return t
            return sb

        def sem(name):
            return ctx.enter_context(nc.semaphore(name))

        top = [(nc.sbuf_base + 31) // 32 * 32]
        sb = stack(top)
        xhi = sb("xhi", [P, KS, TOK], F32R)
        xlo = sb("xlo", [P, KS, TOK], F32R)
        ring0 = top[0]
        whi = [sb(f"whi{i}", [P, KS, P], F32R) for i in range(RING)]
        wlo = [sb(f"wlo{i}", [P, KS, P], F32R) for i in range(RING)]
        wraw = [sb(f"wraw{i}", [P, KS, P]) for i in range(2)]
        rms0 = top[0]
        rms = sb("rms", [P, TOK])
        cst = sb("cst", [P, 3 * P + (2 * LV - 1) * 64])
        ones = sb("ones", [P, P])
        prm = sb("prm", [P, 64])
        gb_col = sb("gb_col", [P, NT, 2, H])
        col = sb("col", [P, 64])
        ident, tri, pair_mask = cst[:, 0:P], cst[:, P:2 * P], cst[:, 2 * P:3 * P]
        inv_mask = cst[:, 3 * P:3 * P + (LV - 1) * 64].rearrange("p (l n) -> p l n", n=64)
        hg_mask = cst[:, 3 * P + (LV - 1) * 64:].rearrange("p (l n) -> p l n", n=64)
        nw, cw = prm[:, 0:KS], prm[:, 8:56].rearrange("p (c j) -> p c j", j=4)
        gnw, hnw, lbl = prm[:, 56:57], prm[:, 57:58], prm[:, 58:62]
        alog, dtb = prm[0:H, 62:63], prm[0:H, 63:64]
        eps, one = col[:, 0:1], col[:, 1:2]
        nega = col[0:H, 2:3]
        lb, omlb, lbe = col[:, 4:8], col[:, 8:12], col[:, 16:20]
        gcs, gle, kdc = col[:, 12:16], col[:, 16:20], col[:, 20:24]
        ssh, rh = col[:, 24:40].rearrange("p (t e) -> p t e", e=2), col[:, 40:48]

        arena = top[0]
        SLOT = 3 * HALF * 4
        X = place("X", [P, 9, 3 * HALF], F32, arena)
        xraw = place("xraw", [P, KS, TOK], F32, arena)
        work = arena + 56 * 1024

        w1 = [work]
        sb = stack(w1)
        pre = sb("pre", [P, 3 + TOK])
        conv = [sb(f"conv{i}", [P, HALF]) for i in range(2)]
        sqx = [sb(f"sqx{i}", [P, TOK]) for i in range(2)]
        sqa = sb("sqa", [P, TOK])
        ab = sb("ab", [64, TOK])
        ab1 = sb("ab1", [H, TOK])
        ab2 = sb("ab2", [H, TOK])
        gb = sb("gb", [64, TOK])

        w2 = [work]
        sb = stack(w2)
        sq = sb("sq", [P, 2, HALF])
        dec = [sb(f"dec{i}", [P, H, P]) for i in range(2)]
        egr = [sb(f"egr{i}", [P, H, P]) for i in range(2)]
        kdec = sb("kdec", [P, H, P])
        vtok = sb("vtok", [P, HALF])
        AT = sb("AT", [P, H, P])
        QK = sb("QK", [P, H, P])
        T = sb("T", [P, H, P])
        TT = sb("TT", [P, H, P])
        X0 = sb("X0", [P, HALF])
        vnew = sb("vnew", [P, H, P])
        S = sb("S", [P, H, P])
        U = [sb(f"U{i}", [P, H, P]) for i in range(1, LV)]

        w3 = [work]
        sb = stack(w3)
        hitok = sb("hitok", [P, NT, H, P])
        w3b = [w3[0]]
        hst = [sb(f"hst{i}", [P, HALF]) for i in range(2)]
        nrm = sb("nrm", [P, HALF])
        sb = stack(w3b)
        QP = [sb(f"QP{i}", [P, H, P]) for i in range(2)]
        KR = [sb(f"KR{i}", [P, H, P]) for i in range(2)]
        FF = [sb(f"FF{i}", [P, H, P]) for i in range(2)]
        TOT = sb("TOT", [P, H * P])
        HA = sb("HA", [P, H, P])
        kdt = sb("kdt", [P, H, P])
        HS = sb("HS", [P, H, P])
        zr = [sb(f"zr{i}", [P, HALF]) for i in range(2)]
        sg = [sb(f"sg{i}", [P, HALF]) for i in range(2)]

        yhi = [place("yahi", [P, H, TOK], F32R, work), place("ybhi", [P, H, TOK], F32R, arena + 4 * SLOT)]
        ylo = [place("yalo", [P, H, TOK], F32R, work + 16384),
               place("yblo", [P, H, TOK], F32R, arena + 4 * SLOT + 16384)]
        mat = [work + 32768, work + 36864] + [arena + 4096 * d for d in range(6)]
        merged = [place(f"merged{d}", [P, TOK], F32, mat[d]) for d in range(KS)]
        gateb = place("gateb", [P, TOK], F32, work + 40960)

        wohi = place("wohi", [P, KS, DM], F32R, work)
        wolo = place("wolo", [P, KS, DM], F32R, arena + 4 * SLOT)
        hat = [base + 4096 * k for base in (work, arena + 4 * SLOT) for k in range(RING)] + [rms0, work + 40960]
        hres = [place(f"hres{t}", [P, DM], F32, hat[t]) for t in range(NT)]
        scr = place("scr", [P, DM], F32, arena)
        fnw = place("fnw", [P, DM], F32, arena + 4096)
        assert max(w1[0], w2[0], w3b[0], work + 45056) <= nc.sbuf_usable_end

        B = [ctx.enter_context(nc.psum_tensor(f"bank{i}", [P, HALF], F32)) for i in range(8)]

        s_prm, s_cst, s_fn = sem("s_prm"), sem("s_cst"), sem("s_fn")
        s_x = [sem(f"x_landed{k}") for k in range(KS)]
        s_w = [sem("w_landed0"), sem("w_landed1")]
        s_res = [sem(f"res_landed{t}") for t in range(NT)]
        x_sq, x_hi, x_lo, sq_added = sem("x_sq"), sem("x_hi"), sem("x_lo"), sem("sq_added")
        ss_done, rms_done = sem("ss_done"), sem("rms_done")
        w_hi, w_lo = sem("w_hi"), sem("w_lo")
        acc_done = sem("acc_done")
        acc_out = [sem("acc_out0"), sem("acc_out1")]
        phase = sem("phase")
        setup = sem("setup")
        dstep, astep, pstep = sem("dstep"), sem("astep"), sem("pstep")
        tap_done, conv_done, silu_done = sem("tap_done"), sem("conv_done"), sem("silu_done")
        ab_row, ab_act, gb_row, gb_turned = sem("ab_row"), sem("ab_act"), sem("gb_row"), sem("gb_turned")
        sq_done, ssq_done, rs_done, qk_norm = sem("sq_done"), sem("ssq_done"), sem("rs_done"), sem("qk_norm")
        gcum_done, gcs_out, dif_done, kv_turned, att_done = (
            sem("gcum_done"), sem("gcs_out"), sem("dif_done"), sem("kv_turned"), sem("att_done"))
        dec_done, egr_done, kdc_done, v_out = sem("dec_done"), sem("egr_done"), sem("kdc_done"), sem("v_out")
        decm_done, kg_done = sem("decm_done"), sem("kg_done")
        tt_first, tt_turned, t_first = sem("tt_first"), sem("tt_turned"), sem("t_first")
        qk_ready, u_psum, u_ready, t_psum, t_ready = (
            sem("qk_ready"), sem("u_psum"), sem("u_ready"), sem("t_psum"), sem("t_ready"))
        tt_psum, tt_ready = sem("tt_psum"), sem("tt_ready")
        kd_ready = sem("kd_ready")
        ks_done, x0_done, tx_done, vn_done = sem("ks_done"), sem("x0_done"), sem("tx_done"), sem("vn_done")
        o_done, su_done, s_ready, oa_out = sem("o_done"), sem("su_done"), sem("s_ready"), sem("oa_out")
        hi_turned, hi_out = sem("hi_turned"), sem("hi_out")
        o_sq, o_ss, o_rs, o_nrm = sem("o_sq"), sem("o_ss"), sem("o_rs"), sem("o_nrm")
        hf_sig, hf_f0, hf_f, hk_lb, qf_done = sem("hf_sig"), sem("hf_f0"), sem("hf_f"), sem("hk_lb"), sem("qf_done")
        hd_psum, hl_psum, q_upd, k_upd = sem("hd_psum"), sem("hl_psum"), sem("q_upd"), sem("k_upd")
        hd_done, ha_done, tot_done = sem("hd_done"), sem("ha_done"), sem("tot_done")
        hk_turned, hk_out, ho_done, hs_done, hs_ready, ob_out = (
            sem("hk_turned"), sem("hk_out"), sem("ho_done"), sem("hs_done"), sem("hs_ready"), sem("ob_out"))
        z_sig, z_y = sem("z_sig"), sem("z_y")
        y_hi, y_lo = sem("y_hi"), sem("y_lo")
        g_sig, m_done = sem("g_sig"), sem("m_done")
        m_hi, m_lo = sem("m_hi"), sem("m_lo")
        out_done, h_res, h_rs, h_out = sem("out_done"), sem("h_res"), sem("h_rs"), sem("h_out")
        stored = sem("stored")

        def rows(t):
            return slice(P * t, P * (t + 1))

        def qkv(t):
            return X[:, t + 1, :].rearrange("p (c n) -> p c n", n=P)

        def blocks(ap, s):
            return ap.rearrange("p h (b e s) -> p (h b) e s", e=2, s=s)

        def packed(ap, s):
            return ap.rearrange("p (b s) -> p b s", s=s)

        def even_odd(ap, s):
            return ap.rearrange("p h (b e s) -> p h b e s", e=2, s=s)

        def mask(m, s):
            return m.rearrange("p (b s) -> p b s", s=s)[:, None, :, :].broadcast_to([P, 2, 64 // s, s])

        def pair(g):
            return slice(2 * g, 2 * g + 2)

        def by_head(ap):
            return ap[:, :, None].broadcast_to([P, H, P])

        def totals(lv, t, g=None):
            if lv == 0:
                tot = FF[t % 2][:].rearrange("p h n -> p (h n)")
            else:
                at = sum(H * P >> i for i in range(1, lv))
                tot = TOT[:, at:at + (H * P >> lv)]
            if g is not None:
                n = 2 * P >> lv
                tot = tot[:, n * g:n * (g + 1)]
            return tot.rearrange("p (b e) -> p b e", e=2)

        def level(t, lv, g):
            return (t * (LV - 1) + lv - 1) * 2 + g + 1

        def turned(t, lv, g):
            return (t * (LV - 2) + lv - 1) * 2 + g + 1

        def hlevel(t, lv, g):
            return (t * LV + lv) * 2 + g + 1

        def out_of_bank(eng, g):
            eng.wait_ge(acc_out[g % 2], g // 2 + 1)

        def leave(eng):
            eng.drain().then_inc(phase, 1)

        def enter(eng, n):
            eng.wait_ge(phase, 4 * n)

        def wout(k):
            if k < RING:
                i = (S_OUT + k) % RING
                return [w[i][:].rearrange("p k n -> p (k n)") for w in (whi, wlo)]
            return wohi[:, k, :], wolo[:, k, :]

        block = ctx.enter_context(nc.Block())

        @block.sync
        def _(sp):
            def load_w(s):
                if s >= 2:
                    sp.wait_ge(w_hi, s - 1)
                    sp.wait_ge(w_lo, s - 1)
                sp.dma_start(wraw[s % 2][:].rearrange("p k n -> p (k n)"), w_tiles[s]).then_inc(s_w[s % 2], 16)

            sp.dma_start(prm[:], params).then_inc(s_prm, 16)
            sp.dma_start(xraw[:, 0, :], xT[0:P, :]).then_inc(s_x[0], 16)
            load_w(0)
            for k in range(1, KS):
                sp.dma_start(xraw[:, k, :], xT[P * k:P * (k + 1), :]).then_inc(s_x[k], 16)
                if k == 4:
                    load_w(1)
            sp.dma_start(cst[:], consts).then_inc(s_cst, 16)
            for s in range(2, NS):
                load_w(s)
            sp.wait_ge(acc_done, ALL_GROUPS)
            sp.wait_ge(m_done, 2 * KS)
            for t in range(NT):
                sp.dma_start(hres[t][:], xtok[rows(t), :]).then_inc(s_res[t], 16)
            sp.wait_ge(m_hi, KS)
            sp.wait_ge(m_lo, KS)
            sp.dma_start(fnw[:], fnorm).then_inc(s_fn, 16)
            for t in range(NT):
                sp.wait_ge(h_out, t + 1)
                sp.dma_start(out[rows(t), :], hres[t][:]).then_inc(stored, 16)
            sp.wait_ge(stored, 16 * NT)

        @block.tensor
        def _(pe):
            def gemm(s, n0=0, n1=2 * MM):
                for n in range(n0, n1):
                    half, m = divmod(n, MM)
                    k, term = divmod(m, 3)
                    g = first_group(s) + half
                    if n == 0:
                        pe.wait_ge(w_hi, s + 1)
                        pe.wait_ge(w_lo, s + 1)
                    if m == 0 and s > S_QKV:
                        pe.wait_ge(acc_out[g % 2], g // 2)
                    w = wlo if term == 2 else whi
                    x = xlo if term == 1 else xhi
                    mm = nc.tensor.matmul(B[g % 2][:], w[s % RING][:, k, :], x[:, k, HALF * half:HALF * (half + 1)],
                                          start=(m == 0), stop=(m == MM - 1))
                    if m == MM - 1:
                        mm.then_inc(acc_done, 1)

            def square_sums(src, banks):
                for i, b in enumerate(banks):
                    mm = nc.tensor.matmul(B[b][:], ones[:], src[:, i, :], start=True, stop=True)
                return mm

            pe.wait_ge(setup, 1)
            pe.wait_ge(w_hi, 1)
            pe.wait_ge(w_lo, 1)
            for k in range(KS):
                pe.wait_ge(x_hi, k + 1)
                pe.wait_ge(x_lo, k + 1)
                for half in range(2):
                    part = slice(HALF * half, HALF * (half + 1))
                    for term in range(3):
                        w = wlo if term == 2 else whi
                        x = xlo if term == 1 else xhi
                        mm = nc.tensor.matmul(B[4 + half][:], w[0][:, k, :], x[:, k, part],
                                              start=(k == 0 and term == 0), stop=(k == KS - 1 and term == 2))
                    if k == KS - 1:
                        mm.then_inc(acc_done, 1)
            gemm(S_QKV, 0, 12)
            for half in range(2):
                pe.wait_ge(sq_added, KS - 1 + half)
                nc.tensor.matmul(B[2 + half][:], ones[:], sqa[:, HALF * half:HALF * (half + 1)],
                                 start=True, stop=True).then_inc(ss_done, 1)
            gemm(S_QKV, 12)
            for s in range(S_QKV + 1, S_HQF):
                for half in range(2):
                    gemm(s, MM * half, MM * (half + 1))
                if s == 4:
                    pe.wait_ge(gb_row, 2)
                    pe.wait_ge(s_cst, 16)
                    for t in range(NT):
                        mm = nc.tensor.transpose(B[4][:, 64 * t:64 * (t + 1)], gb[:, P * t:P * (t + 1)],
                                                 ident[0:64, 0:64])
                    mm.then_inc(gb_turned, 1)
            leave(pe)

            fed = [0] * NT

            def fill(t, n, upto=2 * MM):
                n = min(n, upto - fed[t])
                gemm(S_HQF + t, fed[t], fed[t] + n)
                fed[t] += n

            def norm_sums(t):
                pe.wait_ge(sq_done, t + 1)
                if t:
                    pe.wait_ge(kd_ready, t)
                    pe.wait_ge(v_out, t)
                nc.tensor.matmul(B[4][:], ones[:], sq[:, 1, :], start=True, stop=True).then_inc(ssq_done, 1)
                nc.tensor.matmul(B[2][:], ones[:], sq[:, 0, :], start=True, stop=True).then_inc(ssq_done, 1)

            def decay_sums(t):
                if t:
                    pe.wait_ge(s_ready, t)
                if t >= 2:
                    pe.wait_ge(oa_out, t - 1)
                nc.tensor.matmul(B[3][:, 0:H], tri, gb_col[:, t, 0, :], start=True, stop=True)
                for h in range(H):
                    mm = nc.tensor.matmul(B[5][:, P * h:P * (h + 1)],
                                          gb_col[:, t, 0, h:h + 1].broadcast_to([P, P]), tri, start=True, stop=True)
                mm.then_inc(gcum_done, 1)

            def new_values(t):
                pe.wait_ge(x0_done, t + 1)
                pe.wait_ge(t_ready, level(t, LV - 1, 1))
                for h in range(H):
                    mm = nc.tensor.matmul(B[3][:, P * h:P * (h + 1)], TT[:, h, :], X0[:, P * h:P * (h + 1)],
                                          start=True, stop=True)
                mm.then_inc(tx_done, 1)

            def outputs(t):
                pe.wait_ge(vn_done, t + 1)
                if t < NT - 1:
                    pe.wait_ge(egr_done, t + 2)
                for h in range(H):
                    nc.tensor.matmul(B[5][:, P * h:P * (h + 1)], S[:, h, :], qkv(t)[:, h, :],
                                     start=True, stop=False)
                    mm = nc.tensor.matmul(B[5][:, P * h:P * (h + 1)], vnew[:, h, :], QK[:, h, :],
                                          start=False, stop=True)
                mm.then_inc(o_done, 1)
                for h in range(H):
                    mm = nc.tensor.matmul(B[3][:, P * h:P * (h + 1)], kdec[:, h, :], vnew[:, h, :],
                                          start=True, stop=True)
                mm.then_inc(su_done, 1)

            fill(0, 10)
            norm_sums(0)
            pe.wait_ge(gb_turned, 2)
            decay_sums(0)
            fill(0, 10)
            for t in range(NT):
                last = t == NT - 1
                upto = 2 * MM - (14 if last else 0)
                if t:
                    new_values(t - 1)
                pe.wait_ge(qk_norm, t + 1)
                for h in range(H):
                    both = X[:, t + 1, 0:2 * HALF].rearrange("p (g h n) -> p g h n", g=2, h=H)[:, :, h, :]
                    mm = nc.tensor.matmul(B[6 + h // 2][:, 256 * (h % 2):256 * (h % 2 + 1)],
                                          qkv(t)[:, H + h, :], both, start=True, stop=True)
                mm.then_inc(att_done, 1)
                pe.wait_ge(dif_done, t + 1)
                for i, b in ((1, 2), (2, 4)):
                    for h in range(H):
                        mm = nc.tensor.transpose(B[b][:, P * h:P * (h + 1)], qkv(t)[:, H * i + h, :], ident)
                mm.then_inc(kv_turned, 1)
                fill(t, 3)
                if t:
                    outputs(t - 1)
                fill(t, 6, upto)
                pe.wait_ge(tt_first, t + 1)
                pe.wait_ge(qk_ready, t + 1)
                for h in range(H):
                    mm = nc.tensor.transpose(B[6][:, P * h:P * (h + 1)], TT[:, h, :], ident)
                mm.then_inc(tt_turned, 1)
                fill(t, 3, upto)
                for lv in range(1, LV):
                    s = 1 << lv
                    for g in range(2):
                        if lv == 1:
                            pe.wait_ge(t_first, t + 1)
                        else:
                            pe.wait_ge(t_ready, level(t, lv - 1, g))
                        for i in range(2):
                            h = 2 * g + i
                            mm = nc.tensor.matmul(packed(B[6 + g][:, 64 * i:64 * (i + 1)], s), AT[:, h, :],
                                                  blocks(T[:, h:h + 1, :], s)[:, :, 0, :], start=True, stop=True)
                        mm.then_inc(u_psum, 1)
                        if lv > 1:
                            if lv == 2 and g == 0:
                                pe.wait_ge(s_ready, t + 1)
                            if lv == 3 and g == 0 and not last:
                                pe.wait_ge(gcs_out, t + 2)
                            if lv == 2 and g == 1 and not last:
                                pe.wait_ge(rs_done, 2 * t + 3)
                            for i in range(2):
                                mm = nc.tensor.transpose(B[3 + g][:, P * i:P * (i + 1)], T[:, 2 * g + i, :], ident)
                            mm.then_inc(tt_psum, 1)
                        fill(t, 1, upto)
                    for g in range(2):
                        pe.wait_ge(u_ready, level(t, lv, g))
                        if lv > 1:
                            pe.wait_ge(tt_ready, turned(t, lv - 1, g))
                        for i in range(2):
                            h = 2 * g + i
                            dst = packed(B[6 + g][:, 128 + 64 * i:128 + 64 * (i + 1)], s)
                            if lv < LV - 1:
                                mm = nc.tensor.matmul(dst, TT[:, h, :], blocks(U[lv - 1][:, h:h + 1, :], s)[:, :, 0, :],
                                                      start=True, stop=True)
                            else:
                                mm = nc.tensor.matmul(dst, U[lv - 1][:, h, :], blocks(TT[:, h:h + 1, :], s)[:, :, 1, :],
                                                      start=True, stop=True)
                        mm.then_inc(t_psum, 1)
                        fill(t, 2, upto)
                    if lv == 1 and not last:
                        norm_sums(t + 1)
                    if lv == 2 and not last:
                        decay_sums(t + 1)
                    if lv == 4:
                        pe.wait_ge(kg_done, 2 * (t + 1))
                        pe.wait_ge(s_ready, t + 1)
                        if last:
                            pe.wait_ge(kd_ready, t + 1)
                        else:
                            pe.wait_ge(rs_done, 2 * (t + 2))
                        for h in range(H):
                            mm = nc.tensor.matmul(B[2][:, P * h:P * (h + 1)], qkv(t)[:, H + h, :], S[:, h, :],
                                                  start=True, stop=True)
                        mm.then_inc(ks_done, 1)
                fill(t, 2 * MM, upto)
            fill(NT - 1, 2)
            new_values(NT - 1)
            fill(NT - 1, 6)
            outputs(NT - 1)
            fill(NT - 1, 2 * MM)
            leave(pe)

            for u in range(NT):
                gemm(S_HI + u // 2, MM * (u % 2), MM * (u % 2) + 12)
                pe.wait_ge(o_sq, u + 1)
                if u:
                    pe.wait_ge(o_nrm, u)
                nc.tensor.matmul(B[3][:], ones[:], nrm[:], start=True, stop=True).then_inc(o_ss, 1)
                gemm(S_HI + u // 2, MM * (u % 2) + 12, MM * (u % 2) + 24)
                if u >= 1:
                    turn_hi = u - 1
                    out_of_bank(pe, 2 * S_HI + turn_hi)
                    if turn_hi:
                        pe.wait_ge(hi_out, turn_hi)
                    for i in range(4):
                        mm = nc.tensor.transpose(B[2][:, P * i:P * (i + 1)], hst[turn_hi % 2][:, P * i:P * (i + 1)],
                                                 ident)
                    mm.then_inc(hi_turned, 1)
            gemm(S_ZA, 0, 12)
            out_of_bank(pe, 2 * S_HI + NT - 1)
            pe.wait_ge(hi_out, NT - 1)
            for i in range(4):
                mm = nc.tensor.transpose(B[2][:, P * i:P * (i + 1)], hst[(NT - 1) % 2][:, P * i:P * (i + 1)], ident)
            mm.then_inc(hi_turned, 1)
            leave(pe)

            for t in range(NT):
                fed = [MM * (t % 2) + (12 if t == 0 else 0)]

                def fill(n):
                    n = min(n, MM * (t % 2 + 1) - fed[0])
                    gemm(S_ZA + t // 2, fed[0], fed[0] + n)
                    fed[0] += n

                KRt, QPt = KR[t % 2], QP[t % 2]
                pe.wait_ge(hk_lb, t + 1)
                if t:
                    pe.wait_ge(ob_out, t)
                for h in range(H):
                    mm = nc.tensor.matmul(B[6][:, P * h:P * (h + 1)], KRt[:, h, :], X[:, h, P * t:P * (t + 1)],
                                          start=True, stop=True)
                mm.then_inc(hd_psum, 1)
                fill(1)
                for lv in range(LV):
                    s = 1 << lv
                    for g in range(2):
                        if lv == 0:
                            pe.wait_ge(qf_done, t + 1)
                        else:
                            pe.wait_ge(q_upd, hlevel(t, lv - 1, g))
                            pe.wait_ge(k_upd, hlevel(t, lv - 1, g))
                        if lv >= 2:
                            pe.wait_ge(ha_done, hlevel(t, lv - 2, g))
                        for i in range(2):
                            h = 2 * g + i
                            mm = nc.tensor.matmul(packed(B[2 + 2 * g + lv % 2][:, 64 * i:64 * (i + 1)], s),
                                                  KRt[:, h, :], blocks(QPt[:, h:h + 1, :], s)[:, :, 1, :],
                                                  start=True, stop=True)
                        mm.then_inc(hl_psum, 1)
                        fill(1 + (lv % 2))
                pe.wait_ge(k_upd, hlevel(t, LV - 1, 1))
                pe.wait_ge(hs_ready, t + 1)
                for h in range(H):
                    mm = nc.tensor.transpose(B[7][:, P * h:P * (h + 1)], KRt[:, h, :], ident)
                mm.then_inc(hk_turned, 1)
                fill(1)
                pe.wait_ge(q_upd, hlevel(t, LV - 1, 1))
                pe.wait_ge(ha_done, hlevel(t, LV - 1, 1))
                for h in range(H):
                    nc.tensor.matmul(B[6][:, P * h:P * (h + 1)], HS[:, h, :], QPt[:, h, :], start=True, stop=False)
                    mm = nc.tensor.matmul(B[6][:, P * h:P * (h + 1)], hitok[:, t, h, :], HA[:, h, :],
                                          start=False, stop=True)
                mm.then_inc(ho_done, 1)
                pe.wait_ge(hk_out, t + 1)
                for h in range(H):
                    mm = nc.tensor.matmul(B[7][:, P * h:P * (h + 1)], kdt[:, h, :], hitok[:, t, h, :],
                                          start=True, stop=True)
                mm.then_inc(hs_done, 1)
                fill(24)
            leave(pe)

            for u in range(NT):
                gemm(S_ZB + u // 2, MM * (u % 2), MM * (u % 2) + 12)
                pe.wait_ge(o_sq, NT + u + 1)
                pe.wait_ge(o_nrm, NT + u)
                nc.tensor.matmul(B[3][:], ones[:], nrm[:], start=True, stop=True).then_inc(o_ss, 1)
                gemm(S_ZB + u // 2, MM * (u % 2) + 12, MM * (u % 2) + 24)
            leave(pe)

            for d in range(KS):
                gemm(S_MERGE + 3 * d)
                gemm(S_MERGE + 3 * d + 1)
                s = S_MERGE + 3 * d + 2
                pe.wait_ge(w_hi, s + 1)
                pe.wait_ge(w_lo, s + 1)
                if d == 0:
                    pe.wait_ge(y_hi, 2 * H)
                    pe.wait_ge(y_lo, 2 * H)
                for half in range(2):
                    part = slice(HALF * half, HALF * (half + 1))
                    for br in range(2):
                        g = first_group(s) + 2 * half + br
                        pe.wait_ge(acc_out[g % 2], g // 2)
                        for h in range(H):
                            for term in range(3):
                                w = wlo if term == 2 else whi
                                y = ylo if term == 1 else yhi
                                mm = nc.tensor.matmul(B[g % 2][:], w[s % RING][:, H * br + h, :], y[br][:, h, part],
                                                      start=(h == 0 and term == 0),
                                                      stop=(h == H - 1 and term == 2))
                        mm.then_inc(acc_done, 1)

            def out_product(t, k, e, last):
                hi, lo = wout(k)
                for term in range(3):
                    m = xlo if term == 1 else xhi
                    w = lo if term == 2 else hi
                    mm = nc.tensor.matmul(B[t][:], m[:, k, P * t:P * (t + 1)], w[:, HALF * e:HALF * (e + 1)],
                                          start=(k == 0 and term == 0), stop=(k == KS - 1 and term == 2))
                if last:
                    mm.then_inc(out_done, 1)

            pe.wait_ge(acc_out[0], ALL_GROUPS // 2)
            pe.wait_ge(acc_out[1], ALL_GROUPS // 2)
            for k in range(KS):
                pe.wait_ge(m_hi, k + 1)
                pe.wait_ge(m_lo, k + 1)
                pe.wait_ge(w_hi, S_OUT + k + 1)
                pe.wait_ge(w_lo, S_OUT + k + 1)
                for t in range(NT):
                    out_product(t, k, 0, k == KS - 1)
            for t in range(NT):
                pe.wait_ge(h_res, t + 1)
                for k in range(KS):
                    out_product(t, k, 1, k == KS - 1)

        def split_target(s):
            if s < S_OUT + RING:
                return whi[s % RING][:], wlo[s % RING][:]
            k = s - S_OUT
            cut = "p (k n) -> p k n"
            return wohi[:, k, :].rearrange(cut, k=KS), wolo[:, k, :].rearrange(cut, k=KS)

        def split_waits(eng, s):
            eng.wait_ge(s_w[s % 2], 16 * (s // 2 + 1))
            if s >= S_OUT + RING:
                eng.wait_ge(acc_done, ALL_GROUPS)
            elif s >= RING:
                eng.wait_ge(acc_done, end_group(s - RING))

        @block.scalar
        def _(act):
            def link(ins, n=[0]):
                n[0] += 1
                ins.then_inc(astep, 1)
                act.wait_ge(astep, n[0])

            def split_hi(s):
                split_waits(act, s)
                nc.scalar.activation(split_target(s)[0], wraw[s % 2][:], ACT.Identity).then_inc(w_hi, 1)

            nc.scalar.preload_act_table_set("natural_log_exp_and_others")
            act.wait_ge(setup, 1)
            act.wait_ge(s_prm, 16)
            split_hi(0)
            for k in range(KS):
                act.wait_ge(s_x[k], 16)
                nc.scalar.activation(xhi[:, k, :], xraw[:, k, :], ACT.Identity, scale=nw[:, k:k + 1]).then_inc(x_hi, 1)
                if k >= 2:
                    act.wait_ge(sq_added, k - 1)
                nc.scalar.activation(sqx[k % 2][:], xraw[:, k, :], ACT.Square).then_inc(x_sq, 1)
            split_hi(1)
            for half in range(2):
                act.wait_ge(ss_done, half + 1)
                part = rms[:, HALF * half:HALF * (half + 1)]
                link(nc.scalar.activation(part, B[2 + half][:], ACT.Ln, bias=eps, scale=1.0 / DM))
                nc.scalar.activation(part, part, ACT.Exp, scale=-0.5).then_inc(rms_done, 1)
            nc.scalar.activation(nega, alog, ACT.Exp).then_inc(ab_act, 1)
            act.wait_ge(ab_row, 1)
            nc.scalar.activation(lbe, lbe, ACT.Exp).then_inc(ab_act, 1)
            act.wait_ge(ab_row, 2)
            link(nc.scalar.activation(ab2[:], ab2[:], ACT.Exp))
            nc.scalar.activation(ab2[:], ab2[:], ACT.Ln, bias=one[0:H]).then_inc(ab_act, 1)
            nc.scalar.activation(ab[32:32 + H, :], ab[32:32 + H, :], ACT.Exp, scale=-1.0).then_inc(ab_act, 1)
            split_hi(2)

            def silu(u):
                s, half = S_QKV + u // 2, u % 2
                act.wait_ge(conv_done, u + 1)
                c = s - S_QKV
                dst = X[:, 4 * half + 1:4 * half + 5, P * c:P * (c + 1)]
                nc.scalar.activation(dst, conv[half][:].rearrange("p (t n) -> p t n", n=P),
                                     ACT.Silu).then_inc(silu_done, 1)

            for u in range(2 * (S_HQF - S_QKV)):
                c, half = divmod(u, 2)
                out_of_bank(act, 2 * S_QKV + u)
                if u >= 2:
                    act.wait_ge(silu_done, u - 1)
                nc.scalar.activation(conv[half][:], pre[:, HALF * half:HALF * (half + 1)], ACT.Identity,
                                     scale=cw[:, c, 0:1]).then_inc(tap_done, 1)
                if u:
                    silu(u - 1)
                if half:
                    split_hi(S_QKV + c + 2)
            silu(2 * (S_HQF - S_QKV) - 1)
            leave(act)
            enter(act, 1)

            nc.scalar.preload_act_table_set("natural_log_exp_and_others")

            def squares(t):
                if t:
                    act.wait_ge(qk_norm, t)
                nc.scalar.activation(sq[:].rearrange("p g n -> p (g n)"), X[:, t + 1, 0:2 * HALF],
                                     ACT.Square).then_inc(sq_done, 1)

            def norm(t, i):
                act.wait_ge(ssq_done, 2 * (t + 1) - i)
                link(nc.scalar.activation(sq[:, i, :], B[2 + 2 * i][:], ACT.Ln, bias=eps))
                nc.scalar.activation(sq[:, i, :], sq[:, i, :], ACT.Exp, scale=-0.5).then_inc(rs_done, 1)

            def turned_t(t, lv):
                for g in range(2):
                    act.wait_ge(tt_psum, turned(t, lv, g))
                    nc.scalar.activation(TT[:, pair(g), :].rearrange("p h n -> p (h n)"), B[3 + g][:, 0:256],
                                         ACT.Identity).then_inc(tt_ready, 1)

            def decays(t):
                act.wait_ge(dif_done, t + 1)
                nc.scalar.activation(dec[t % 2][:], dec[t % 2][:], ACT.Exp).then_inc(dec_done, 1)
                nc.scalar.activation(egr[t % 2][:].rearrange("p h n -> p (h n)"), B[5][:], ACT.Exp).then_inc(egr_done, 1)
                nc.scalar.activation(kdc, gle, ACT.Exp).then_inc(kdc_done, 1)

            squares(0)
            norm(0, 1)
            norm(0, 0)
            decays(0)
            for t in range(NT + 1):
                if t < NT:
                    act.wait_ge(kv_turned, t + 1)
                    nc.scalar.activation(vtok[:], B[4][:], ACT.Identity).then_inc(v_out, 1)
                if t:
                    act.wait_ge(o_done, t)
                    nc.scalar.activation(X[:, t - 1, 2 * HALF:3 * HALF], B[5][:], ACT.Identity).then_inc(oa_out, 1)
                if t < NT:
                    act.wait_ge(tt_turned, t + 1)
                    nc.scalar.activation(T[:].rearrange("p h n -> p (h n)"), B[6][:], ACT.Identity).then_inc(t_first, 1)
                if t < NT - 1:
                    squares(t + 1)
                for lv in range(1, LV - 1 if t < NT else 1):
                    if lv == 1 and t < NT - 1:
                        norm(t + 1, 1)
                    turned_t(t, lv)
                    if lv == 1 and t < NT - 1:
                        norm(t + 1, 0)
                    if lv == 3:
                        split_hi(S_HQF + t + 2)
                    if lv == 4 and t < NT - 1:
                        decays(t + 1)
            leave(act)
            enter(act, 2)

            def out_squares(u, src):
                if u:
                    act.wait_ge(o_nrm, u)
                nc.scalar.activation(nrm[:].rearrange("p (a b) -> p a b", b=P), src, ACT.Square).then_inc(o_sq, 1)
                act.wait_ge(o_ss, u + 1)
                link(nc.scalar.activation(nrm[:], B[3][:], ACT.Ln, bias=eps, scale=1.0 / P))
                nc.scalar.activation(nrm[:], nrm[:], ACT.Exp, scale=-0.5).then_inc(o_rs, 1)

            def hi_copy(u):
                act.wait_ge(hi_turned, u + 1)
                c, half = divmod(u, 2)
                nc.scalar.activation(hitok[:, 4 * half:4 * half + 4, c, :],
                                     B[2][:].rearrange("p (t n) -> p t n", n=P), ACT.Identity).then_inc(hi_out, 1)

            for u in range(NT):
                out_squares(u, X[:, u, 2 * HALF:3 * HALF].rearrange("p (a b) -> p a b", b=P))
                if u % 2:
                    split_hi(S_HI + u // 2 + 2)
                if u:
                    hi_copy(u - 1)
            hi_copy(NT - 1)
            leave(act)
            enter(act, 3)

            def z_gate(u):
                out_of_bank(act, 2 * S_ZA + u)
                nc.scalar.activation(sg[u % 2][:], zr[u % 2][:], ACT.Sigmoid).then_inc(z_sig, 1)

            def forget(t):
                tile = X[:, 4:8, P * t:P * (t + 1)]
                if t >= 2:
                    act.wait_ge(hk_turned, t - 1)
                nc.scalar.activation(KR[t % 2][:], tile, ACT.Sigmoid, scale=-1.0).then_inc(hf_sig, 1)
                nc.scalar.activation(FF[t % 2][:], tile, ACT.Sigmoid).then_inc(hf_sig, 1)

            forget(0)
            for t in range(NT):
                if t < NT - 1:
                    forget(t + 1)
                if t:
                    z_gate(t - 1)
                if t % 2:
                    split_hi(S_ZA + t // 2 + 2)
                act.wait_ge(hk_turned, t + 1)
                nc.scalar.activation(kdt[:].rearrange("p h n -> p (h n)"), B[7][:], ACT.Identity).then_inc(hk_out, 1)
                act.wait_ge(ho_done, t + 1)
                nc.scalar.activation(X[:, 0:4, P * t:P * (t + 1)], B[6][:].rearrange("p (h n) -> p h n", n=P),
                                     ACT.Identity).then_inc(ob_out, 1)
            z_gate(NT - 1)
            leave(act)
            enter(act, 4)

            for u in range(NT):
                nc.scalar.preload_act_table_set("natural_log_exp_and_others")
                out_squares(NT + u, X[:, u // 2, HALF * (u % 2):HALF * (u % 2 + 1)].rearrange("p (a b) -> p a b", b=P))
                if u % 2:
                    split_hi(S_ZB + u // 2 + 2)
                z_gate(NT + u)
            leave(act)
            enter(act, 5)

            for h in range(H):
                nc.scalar.activation(yhi[0][:, h, :].rearrange("p (t n) -> p t n", n=P),
                                     X[:, 0:NT, 2 * HALF + P * h:2 * HALF + P * (h + 1)], ACT.Identity).then_inc(y_hi, 1)
            act.wait_ge(y_lo, H)
            for h in range(H):
                nc.scalar.activation(yhi[1][:, h, :], X[:, h, 0:TOK], ACT.Identity).then_inc(y_hi, 1)
            for d in range(KS):
                for r in range(2):
                    for half in range(2):
                        out_of_bank(act, first_group(S_MERGE + 3 * d + r) + half)
                        buf = (gateb if r else merged[d])[:, HALF * half:HALF * (half + 1)]
                        nc.scalar.activation(buf, buf, ACT.Sigmoid).then_inc(g_sig, 1)
                    if d < KS - 1 or r == 0:
                        split_hi(S_MERGE + 3 * d + r + 2)
                if d < KS - 1:
                    split_hi(S_MERGE + 3 * d + 4)
            act.wait_ge(acc_done, first_group(S_OUT - 1))
            for k in range(KS):
                act.wait_ge(m_done, 2 * (k + 1))
                nc.scalar.activation(xhi[:, k, :], merged[k][:], ACT.Identity).then_inc(m_hi, 1)
                if k == KS - 2:
                    split_hi(S_OUT)
            for k in range(1, KS):
                split_hi(S_OUT + k)
            nc.scalar.preload_act_table_set("natural_log_exp_and_others")
            for t in range(NT):
                act.wait_ge(h_res, NT + t + 1)
                link(nc.scalar.activation(scr[:], hres[t][:], ACT.Square, accum_out=ssh[:, t, 0:1]))
                link(nc.scalar.activation(rh[:, t:t + 1], ssh[:, t, 0:1], ACT.Ln, bias=eps, scale=1.0 / DM))
                nc.scalar.activation(rh[:, t:t + 1], rh[:, t:t + 1], ACT.Exp, scale=-0.5).then_inc(h_rs, 1)

        @block.gpsimd
        def _(pool):
            def split_lo(s):
                split_waits(pool, s)
                pool.wait_ge(w_hi, s + 1)
                hi, lo = split_target(s)
                nc.gpsimd.tensor_tensor(lo, wraw[s % 2][:], hi.bitcast(F32), ALU.subtract).then_inc(w_lo, 1)

            nc.gpsimd.memset(ones[:], 1.0)
            nc.gpsimd.memset(one, 1.0)
            nc.gpsimd.memset(eps, EPS).then_inc(setup, 1)
            for s in range(S_HQF + 2):
                split_lo(s)
            leave(pool)
            enter(pool, 1)
            for u in U:
                nc.gpsimd.memset(u[:], 0.0)
            nc.gpsimd.memset(S[:], 0.0).then_inc(s_ready, 1)

            def mask_decays(t):
                pool.wait_ge(dec_done, t + 1)
                nc.gpsimd.tensor_tensor(dec[t % 2][:], dec[t % 2][:], tri[:, None, :].broadcast_to([P, H, P]),
                                        ALU.mult).then_inc(decm_done, 1)

            mask_decays(0)
            for t in range(NT):
                pool.wait_ge(egr_done, t + 1)
                pool.wait_ge(kv_turned, t + 1)
                for i in (1, 0):
                    part = X[:, t + 1, HALF * i:HALF * (i + 1)]
                    nc.gpsimd.tensor_tensor(part, part, egr[t % 2][:].rearrange("p h n -> p (h n)"),
                                            ALU.mult).then_inc(kg_done, 1)
                split_lo(S_HQF + t + 2)
                if t < NT - 1:
                    mask_decays(t + 1)
            leave(pool)
            enter(pool, 2)
            for u in range(NT):
                if u % 2:
                    split_lo(S_HI + u // 2 + 2)
            leave(pool)
            enter(pool, 3)
            nc.gpsimd.memset(HS[:], 0.0).then_inc(hs_ready, 1)

            def z_apply(u):
                c, half = divmod(u % NT, 2)
                if u < NT:
                    o = X[:, 4 * half:4 * half + 4, 2 * HALF + P * c:2 * HALF + P * (c + 1)]
                else:
                    o = X[:, c, HALF * half:HALF * (half + 1)].rearrange("p (a b) -> p a b", b=P)
                pool.wait_ge(z_sig, u + 1)
                z3 = zr[u % 2][:].rearrange("p (a b) -> p a b", b=P)
                nc.gpsimd.tensor_tensor(z3, z3, sg[u % 2][:].rearrange("p (a b) -> p a b", b=P),
                                        ALU.mult).then_inc(pstep, 1)
                pool.wait_ge(pstep, u + 1)
                if u >= NT:
                    pool.wait_ge(o_nrm, u + 1)
                nc.gpsimd.tensor_tensor(o, o, z3, ALU.mult).then_inc(z_y, 1)

            def complement(t):
                pool.wait_ge(hf_sig, 2 * t + 1)
                nc.gpsimd.tensor_tensor(KR[t % 2][:], KR[t % 2][:], by_head(omlb), ALU.mult).then_inc(hk_lb, 1)

            complement(0)
            for t in range(NT):
                pool.wait_ge(hf_f, t + 1)
                for lv in range(LV):
                    s = 1 << lv
                    if lv:
                        pool.wait_ge(tot_done, LV * t + lv)
                    for g in range(2):
                        pool.wait_ge(hl_psum, hlevel(t, lv, g))
                        k_even = blocks(KR[t % 2][:, pair(g), :], s)[:, :, 0, :]
                        nc.gpsimd.tensor_tensor(k_even, k_even,
                                                totals(lv, t, g)[:, :, 1:2].broadcast_to([P, 128 // s, s]),
                                                ALU.mult).then_inc(k_upd, 1)
                    if lv == 2 and t < NT - 1:
                        complement(t + 1)
                if t % 2:
                    split_lo(S_ZA + t // 2 + 2)
                if t:
                    z_apply(t - 1)
            z_apply(NT - 1)
            leave(pool)
            enter(pool, 4)
            for u in range(NT):
                if u % 2:
                    split_lo(S_ZB + u // 2 + 2)
                z_apply(NT + u)
            leave(pool)
            enter(pool, 5)
            for s in range(S_MERGE + 2, NS):
                split_lo(s)

        @block.vector
        def _(dve):
            V = nc.vector
            steps = [0]

            def link(ins):
                steps[0] += 1
                ins.then_inc(dstep, 1)
                dve.wait_ge(dstep, steps[0])

            def take(g, dst, rows_=P):
                dve.wait_ge(acc_done, g + 1)
                half = g % 2
                r = rms[0:rows_, HALF * half:HALF * (half + 1)]
                b = B[half + (4 if g < 2 else 0)][0:rows_, :]
                if len(dst.shape) == 3:
                    r, b = (a.rearrange("p (t n) -> p t n", n=P) for a in (r, b))
                V.tensor_tensor(dst, b, r, ALU.mult).then_inc(acc_out[half], 1)

            dve.wait_ge(s_prm, 16)
            V.memset(pre[:, 0:3], 0.0)
            link(V.memset(gb[:], 0.0))
            V.tensor_tensor(lbe, lbl, lbl, ALU.subtract).then_inc(ab_row, 1)
            for k in range(KS):
                dve.wait_ge(x_hi, k + 1)
                V.scalar_tensor_tensor(out=xlo[:, k, :], in0=xraw[:, k, :], scalar=nw[:, k:k + 1],
                                       in1=xhi[:, k, :].bitcast(F32), op0=ALU.mult,
                                       op1=ALU.subtract).then_inc(x_lo, 1)
                if k:
                    dve.wait_ge(x_sq, k + 1)
                    if k >= 2:
                        dve.wait_ge(sq_added, k - 1)
                    for half in range(2 if k == KS - 1 else 1):
                        part = slice(HALF * half, HALF * (half + 1)) if k == KS - 1 else slice(0, TOK)
                        before = sqa if k >= 2 else sqx[0]
                        V.tensor_tensor(sqa[:, part], before[:, part], sqx[k % 2][:, part],
                                        ALU.add).then_inc(sq_added, 1)
            dve.wait_ge(rms_done, 2)
            take(0, ab[:, 0:HALF], 64)
            take(1, ab[:, HALF:TOK], 64)

            def decays(n):
                if n == 0:
                    dve.wait_ge(acc_out[0], 1)
                    dve.wait_ge(acc_out[1], 1)
                    V.tensor_scalar(ab1[:], ab[0:H, :], dtb, 0.0, ALU.add, ALU.max)
                    link(V.tensor_scalar(ab2[:], ab[0:H, :], dtb, None, ALU.add))
                    link(V.tensor_scalar(gb[0:H, :], ab2[:], -1.0, None, ALU.mult))
                    V.tensor_tensor(ab2[:], ab2[:], gb[0:H, :], ALU.min).then_inc(ab_row, 1)
                elif n == 1:
                    dve.wait_ge(ab_act, 1)
                    link(V.tensor_scalar(nega, nega, -1.0, None, ALU.mult))
                    dve.wait_ge(ab_act, 3)
                    link(V.tensor_tensor(ab1[:], ab1[:], ab2[:], ALU.add))
                    V.tensor_scalar(gb[0:H, :], ab1[:], nega, None, ALU.mult).then_inc(gb_row, 1)
                elif n == 2:
                    dve.wait_ge(ab_act, 4)
                    link(V.tensor_scalar(ab[32:32 + H, :], ab[32:32 + H, :], 1.0, None, ALU.add))
                    V.reciprocal(gb[32:32 + H, :], ab[32:32 + H, :]).then_inc(gb_row, 1)
                elif n == 3:
                    link(V.reciprocal(lb, lbe))
                    link(V.tensor_tensor(lbe, lbe, lb, ALU.mult))
                    link(V.tensor_tensor(lb, lbe, lbe, ALU.subtract))
                    V.tensor_scalar(omlb, lb, -1.0, 1.0, ALU.mult, ALU.add)
                elif n == 8:
                    dve.wait_ge(gb_turned, 1)
                    V.tensor_copy(gb_col[:], B[4][:].rearrange("p (t e n) -> p t e n", t=NT, n=32)[:, :, :, 0:H]
                                  ).then_inc(gb_turned, 1)

            decays(0)
            for u in range(2 * (S_HQF - S_QKV)):
                c, half = divmod(u, 2)
                if u:
                    dve.wait_ge(conv_done, u)
                take(2 * S_QKV + u, pre[:, 3 + HALF * half:3 + HALF * (half + 1)])
                dve.wait_ge(tap_done, u + 1)
                for j in range(1, 4):
                    ins = V.scalar_tensor_tensor(out=conv[half][:], in0=pre[:, HALF * half + j:HALF * (half + 1) + j],
                                                 scalar=cw[:, c, j:j + 1], in1=conv[half][:], op0=ALU.mult,
                                                 op1=ALU.add)
                    if j < 3:
                        link(ins)
                ins.then_inc(conv_done, 1)
                if u:
                    decays(u)
            leave(dve)
            enter(dve, 1)

            def norm_q(t):
                dve.wait_ge(rs_done, 2 * t + 2)
                q = X[:, t + 1, 0:HALF]
                V.scalar_tensor_tensor(out=q, in0=q, scalar=QSCALE, in1=sq[:, 0, :], op0=ALU.mult,
                                       op1=ALU.mult).then_inc(qk_norm, 1)

            def norm_k(t):
                dve.wait_ge(rs_done, 2 * t + 1)
                k = X[:, t + 1, HALF:2 * HALF]
                V.tensor_tensor(k, k, sq[:, 1, :], ALU.mult)

            def differences(t, heads, last):
                dve.wait_ge(gcum_done, t + 1)
                if not last:
                    V.tensor_copy(gcs, B[3][:, 0:H]).then_inc(gcs_out, 1)
                    dve.wait_ge(gcs_out, t + 1)
                for h in heads:
                    V.tensor_scalar(dec[t % 2][:, h, :], B[5][:, P * h:P * (h + 1)], gcs[:, h:h + 1], 0.0,
                                    ALU.subtract, ALU.min)
                if last:
                    V.tensor_tensor(gle, B[5][:].rearrange("p (h n) -> p h n", n=P)[:, :, P - 1], gcs,
                                    ALU.subtract).then_inc(dif_done, 1)

            def new_values(t):
                dve.wait_ge(tx_done, t + 1)
                V.tensor_tensor(vnew[:], B[3][:].rearrange("p (h n) -> p h n", n=P), by_head(gb_col[:, t, 1, :]),
                                ALU.mult).then_inc(vn_done, 1)

            def new_state(t):
                dve.wait_ge(su_done, t + 1)
                for h in range(H):
                    ins = V.scalar_tensor_tensor(out=S[:, h, :], in0=S[:, h, :], scalar=egr[t % 2][:, h, P - 1:P],
                                                 in1=B[3][:, P * h:P * (h + 1)], op0=ALU.mult, op1=ALU.add)
                ins.then_inc(s_ready, 1)

            norm_k(0)
            norm_q(0)
            differences(0, (0, 1), False)
            differences(0, (2, 3), True)
            for t in range(NT):
                if t:
                    new_values(t - 1)
                dve.wait_ge(att_done, t + 1)
                dve.wait_ge(decm_done, t + 1)
                for h in range(H):
                    ins = V.scalar_tensor_tensor(out=AT[:, h, :],
                                                 in0=B[6 + h // 2][:, 256 * (h % 2) + P:256 * (h % 2) + 2 * P],
                                                 scalar=gb_col[:, t, 1, h:h + 1], in1=dec[t % 2][:, h, :],
                                                 op0=ALU.mult, op1=ALU.mult)
                link(ins)
                link(V.tensor_tensor(TT[:], AT[:], pair_mask[:, None, :].broadcast_to([P, H, P]), ALU.mult))
                V.tensor_tensor(TT[:], TT[:], ident[:, None, :].broadcast_to([P, H, P]), ALU.add).then_inc(tt_first, 1)
                if t:
                    dve.wait_ge(o_done, t)
                for i in range(2):
                    ins = V.tensor_tensor(QK[:, 2 * i:2 * i + 2, :],
                                          B[6 + i][:].rearrange("p (h n) -> p h n", n=2 * P)[:, :, 0:P],
                                          dec[t % 2][:, 2 * i:2 * i + 2, :], ALU.mult)
                ins.then_inc(qk_ready, 1)
                if t:
                    new_state(t - 1)
                dve.wait_ge(kv_turned, t + 1)
                dve.wait_ge(kdc_done, t + 1)
                V.tensor_tensor(kdec[:], B[2][:].rearrange("p (h n) -> p h n", n=P), by_head(kdc),
                                ALU.mult).then_inc(kd_ready, 1)
                for lv in range(1, LV):
                    s = 1 << lv
                    for g in range(2):
                        dve.wait_ge(u_psum, level(t, lv, g))
                        V.tensor_tensor(even_odd(U[lv - 1][:, pair(g), :], s)[:, :, :, 0, :],
                                        B[6 + g][:, 0:128].rearrange("p (h b s) -> p h b s", h=2, s=s),
                                        mask(inv_mask[:, lv - 1, :], s), ALU.mult).then_inc(u_ready, 1)
                    for g in range(2):
                        dve.wait_ge(t_psum, level(t, lv, g))
                        if lv < LV - 1:
                            part = blocks(T[:, pair(g), :], s)[:, :, 0, :]
                        else:
                            part = blocks(TT[:, pair(g), :], s)[:, :, 1, :]
                        V.tensor_tensor(part, packed(B[6 + g][:, 128:256], s), part, ALU.add).then_inc(t_ready, 1)
                    if t < NT - 1:
                        if lv == 2:
                            differences(t + 1, (0, 1), False)
                        if lv == 3:
                            differences(t + 1, (2, 3), True)
                            norm_k(t + 1)
                        if lv == 4:
                            norm_q(t + 1)
                    if lv == 4:
                        take(2 * (S_HQF + t), X[:, t, 0:HALF])
                    if lv == 5:
                        dve.wait_ge(ks_done, t + 1)
                        dve.wait_ge(v_out, t + 1)
                        V.tensor_tensor(X0[:], vtok[:], B[2][:], ALU.subtract).then_inc(x0_done, 1)
                if t < NT - 1:
                    take(2 * (S_HQF + t) + 1, X[:, t, HALF:TOK])
            new_values(NT - 1)
            new_state(NT - 1)
            take(2 * (S_HQF + NT - 1) + 1, X[:, NT - 1, HALF:TOK])
            leave(dve)
            enter(dve, 2)

            for u in range(NT):
                if u >= 2:
                    dve.wait_ge(hi_turned, u - 1)
                take(2 * S_HI + u, hst[u % 2][:])
                dve.wait_ge(o_rs, u + 1)
                o = X[:, u, 2 * HALF:3 * HALF]
                V.scalar_tensor_tensor(out=o, in0=o, scalar=gnw, in1=nrm[:], op0=ALU.mult,
                                       op1=ALU.mult).then_inc(o_nrm, 1)
            leave(dve)
            enter(dve, 3)

            def take_z(u):
                if u >= 2:
                    dve.wait_ge(z_y, u - 1)
                take(2 * S_ZA + u, zr[u % 2][:])

            def forget(t, part):
                f = FF[t % 2]
                if part == 0:
                    dve.wait_ge(hf_sig, 2 * (t + 1))
                    V.tensor_tensor(f[:], f[:], by_head(omlb), ALU.mult).then_inc(hf_f0, 1)
                elif part == 1:
                    dve.wait_ge(hf_f0, t + 1)
                    V.tensor_tensor(f[:], f[:], by_head(lb), ALU.add).then_inc(hf_f, 1)
                else:
                    if t >= 2:
                        dve.wait_ge(ho_done, t - 1)
                    dve.wait_ge(hf_f, t + 1)
                    V.tensor_tensor(QP[t % 2][:], X[:, 0:H, P * t:P * (t + 1)], f[:], ALU.mult).then_inc(qf_done, 1)

            def new_hstate(t):
                dve.wait_ge(hs_done, t + 1)
                for h in range(H):
                    ins = V.scalar_tensor_tensor(out=HS[:, h, :], in0=HS[:, h, :], scalar=TOT[:, 504 + h:505 + h],
                                                 in1=B[7][:, P * h:P * (h + 1)], op0=ALU.mult, op1=ALU.add)
                ins.then_inc(hs_ready, 1)

            for part in range(3):
                forget(0, part)
            for t in range(NT):
                dve.wait_ge(hd_psum, t + 1)
                V.tensor_tensor(HA[:], B[6][:].rearrange("p (h n) -> p h n", n=P),
                                ident[:, None, :].broadcast_to([P, H, P]), ALU.mult).then_inc(hd_done, 1)
                for lv in range(LV):
                    s = 1 << lv
                    if lv:
                        dve.wait_ge(tot_done, LV * t + lv)
                    tot = totals(lv, t)
                    if lv == LV - 1:
                        dst = TOT[:, 504:508]
                    else:
                        dst = totals(lv + 1, t).rearrange("p b e -> p (b e)")
                    V.tensor_tensor(dst, tot[:, :, 0], tot[:, :, 1], ALU.mult).then_inc(tot_done, 1)
                    for g in range(2):
                        dve.wait_ge(hl_psum, hlevel(t, lv, g))
                        q_odd = blocks(QP[t % 2][:, pair(g), :], s)[:, :, 1, :]
                        V.tensor_tensor(q_odd, q_odd, totals(lv, t, g)[:, :, 0:1].broadcast_to([P, 128 // s, s]),
                                        ALU.mult).then_inc(q_upd, 1)
                    for g in range(2):
                        if lv:
                            dve.wait_ge(ha_done, hlevel(t, lv - 1, g))
                        else:
                            dve.wait_ge(hd_done, t + 1)
                        V.copy_predicated(even_odd(HA[:, pair(g), :], s)[:, :, :, 1, :],
                                          mask(hg_mask[:, lv, :].bitcast(I32), s),
                                          B[2 + 2 * g + lv % 2][:, 0:128].rearrange("p (h b s) -> p h b s", h=2, s=s)
                                          ).then_inc(ha_done, 1)
                    if lv == 1 and t:
                        new_hstate(t - 1)
                    if 2 <= lv <= 4 and t < NT - 1:
                        forget(t + 1, lv - 2)
                    if lv == 5 and t:
                        take_z(t - 1)
            new_hstate(NT - 1)
            take_z(NT - 1)
            leave(dve)
            enter(dve, 4)

            for u in range(NT):
                take_z(NT + u)
                dve.wait_ge(o_rs, NT + u + 1)
                o = X[:, u // 2, HALF * (u % 2):HALF * (u % 2 + 1)]
                V.scalar_tensor_tensor(out=o, in0=o, scalar=hnw, in1=nrm[:], op0=ALU.mult,
                                       op1=ALU.mult).then_inc(o_nrm, 1)
            leave(dve)
            enter(dve, 5)

            def split_y(br, h):
                dve.wait_ge(y_hi, H * br + h + 1)
                if br:
                    y, cut = X[:, h, 0:TOK], "p n -> p n"
                    hi, lo = yhi[br][:, h, :], ylo[br][:, h, :]
                else:
                    y = X[:, 0:NT, 2 * HALF + P * h:2 * HALF + P * (h + 1)]
                    hi, lo = (a[:, h, :].rearrange("p (t n) -> p t n", n=P) for a in (yhi[br], ylo[br]))
                V.tensor_tensor(lo, y, hi.bitcast(F32), ALU.subtract).then_inc(y_lo, 1)

            def take_gate(d, r, half):
                take(first_group(S_MERGE + 3 * d + r) + half,
                     (gateb if r else merged[d])[:, HALF * half:HALF * (half + 1)])

            for h in range(H):
                split_y(0, h)
            take_gate(0, 0, 0)
            for h in range(2):
                split_y(1, h)
            take_gate(0, 0, 1)
            for h in range(2, H):
                split_y(1, h)
            for d in range(KS):
                for r in range(2):
                    for half in range(2):
                        if d:
                            dve.wait_ge(m_done, 2 * d)
                        if d or r:
                            take_gate(d, r, half)
                if d == KS - 1:
                    dve.wait_ge(acc_done, first_group(S_OUT - 1))
                    for k in range(KS - 1):
                        dve.wait_ge(m_hi, k + 1)
                        V.tensor_tensor(xlo[:, k, :], merged[k][:], xhi[:, k, :].bitcast(F32),
                                        ALU.subtract).then_inc(m_lo, 1)
                for half in range(2):
                    part = slice(HALF * half, HALF * (half + 1))
                    dve.wait_ge(g_sig, 4 * (d + 1))
                    for br, gate in ((0, merged[d]), (1, gateb)):
                        g = first_group(S_MERGE + 3 * d + 2) + 2 * half + br
                        dve.wait_ge(acc_done, g + 1)
                        V.tensor_tensor(gate[:, part], B[g % 2][:], gate[:, part], ALU.mult).then_inc(acc_out[g % 2], 1)
                        out_of_bank(dve, g)
                    V.tensor_tensor(merged[d][:, part], merged[d][:, part], gateb[:, part],
                                    ALU.add).then_inc(m_done, 1)
            dve.wait_ge(m_hi, KS)
            V.tensor_tensor(xlo[:, KS - 1, :], merged[KS - 1][:], xhi[:, KS - 1, :].bitcast(F32),
                            ALU.subtract).then_inc(m_lo, 1)
            for e in range(2):
                for t in range(NT):
                    if e == 0:
                        dve.wait_ge(s_res[t], 16)
                    dve.wait_ge(out_done, NT * e + t + 1)
                    part = hres[t][:, HALF * e:HALF * (e + 1)]
                    V.tensor_tensor(part, B[t][:], part, ALU.add).then_inc(h_res, 1)
                    if e:
                        if t == 0:
                            dve.wait_ge(s_fn, 16)
                        dve.wait_ge(h_rs, t + 1)
                        V.scalar_tensor_tensor(out=hres[t][:], in0=hres[t][:], scalar=rh[:, t:t + 1], in1=fnw[:],
                                               op0=ALU.mult, op1=ALU.mult).then_inc(h_out, 1)


def level_masks():
    import numpy as np
    inv = np.zeros((P, LV - 1, 64), np.float32)
    hg = np.zeros((P, LV, 64), np.float32)
    for lv in range(LV):
        s = 1 << lv
        for c in range(64):
            first = c // s * 2 * s
            if lv:
                inv[first + s:first + 2 * s, lv - 1, c] = -1.0
            hg[first:first + s, lv, c] = 1.0
    pairs = np.zeros((P, P), np.float32)
    pairs[np.arange(0, P, 2), np.arange(1, P, 2)] = -1.0
    return pairs, inv.reshape(P, -1), hg.reshape(P, -1)


def kernel(**inputs):
    import numpy as np
    import concourse.bacc as bacc
    from concourse.bass_utils import run_bass_kernel_spmd

    a = {k: np.asarray(v) for k, v in inputs.items()}
    f = np.float32
    x = np.ascontiguousarray(a["x"][0])
    w_in = a["w_in"][0]
    qk, v, heads, wide = H * P, H * P, H, H * P
    cuts = np.cumsum([2 * qk + v, heads, heads, v, wide, wide, wide, wide])
    c_qkv, c_a, c_b, c_za, c_hq, c_hf, c_hi, c_zb, c_gate = np.split(w_in, cuts, axis=1)
    w_ab = np.zeros((DM, P), f)
    w_ab[:, 0:H], w_ab[:, 32:32 + H] = c_a, c_b
    gate_a, gate_b = np.split(c_gate, 2, axis=1)

    def tiles(w):
        return list(w.reshape(w.shape[0] // P, P, w.shape[1] // P, P).transpose(2, 1, 0, 3))

    order = [*tiles(w_ab), *tiles(c_qkv), *tiles(c_hq), *tiles(c_hf), *tiles(c_hi), *tiles(c_za), *tiles(c_zb)]
    branches = a["w_branch"][0].reshape(2 * H * P, DM)
    for g0, g1, br in zip(tiles(gate_a), tiles(gate_b), tiles(branches)):
        order += [g0, g1, br]
    order += list(a["w_out"][0].reshape(KS, P, KS, P))
    w_tiles = np.ascontiguousarray(np.stack(order)).reshape(NS, P, KS * P)

    params = np.zeros((P, 64), f)
    params[:, 0:KS] = a["norm_w"][0].reshape(KS, P).T
    params[:, 8:56] = a["conv_w"][0].reshape(4, 12, P).transpose(2, 1, 0).reshape(P, 48)
    params[:, 56], params[:, 57] = a["gdn_norm_w"][0], a["hg_norm_w"][0]
    params[:, 58:62] = a["hg_lb_logits"][0].reshape(H, P).T
    params[0:H, 62], params[0:H, 63] = a["a_log"][0], a["dt_bias"][0]
    consts = np.concatenate([np.eye(P, dtype=f), np.triu(np.ones((P, P), f)), *level_masks()], axis=1)

    nc = bacc.Bacc("TRN2", target_bir_lowering=False, num_devices=1)
    arrays = {"xT": np.ascontiguousarray(x.T), "xtok": x, "w_tiles": w_tiles, "params": params,
              "fnorm": np.ascontiguousarray(np.broadcast_to(a["final_norm_w"], (P, DM))), "consts": consts}
    aps = [nc.dram_tensor(n, v.shape, mybir.dt.from_np(v.dtype), kind="ExternalInput").ap()
           for n, v in arrays.items()]
    out = nc.dram_tensor("out", (TOK, DM), F32, kind="ExternalOutput").ap()
    bass_hybrid_gdn_hgrn2(nc, *aps, out)
    r = run_bass_kernel_spmd(nc, [arrays], core_ids=[0])
    return r.results[0]["out"].reshape(1, TOK, DM)
```

```python
from contextlib import ExitStack

import concourse.bass as bass
from concourse import mybir

F32 = mybir.dt.float32
F32R = mybir.dt.float32r
I32 = mybir.dt.int32
ALU = mybir.AluOpType
ACT = mybir.ActivationFunctionType

P = 128
TOK = 1024
DM = 1024
NT = TOK // P
KS = DM // P
H = 4
HALF = 512
EPS = 1e-6
LV = 7
QSCALE = float(P) ** -0.5
MM = 3 * KS

S_AB, S_QKV, S_HQF, S_HI, S_ZA, S_ZB, S_MERGE = 0, 1, 13, 21, 25, 29, 33
S_OUT = S_MERGE + 3 * KS
NS = S_OUT + KS
RING = 3


def first_group(s):
    if s < S_MERGE:
        return 2 * s
    d, r = divmod(s - S_MERGE, 3)
    return 2 * S_MERGE + 8 * d + 2 * r


def end_group(s):
    return first_group(s + 1)


ALL_GROUPS = first_group(S_OUT)


def bass_hybrid_gdn_hgrn2(nc, xT, xtok, w_tiles, params, fnorm, consts, out):
    with ExitStack() as ctx:
        def place(name, shape, dt, offset):
            return nc.alloc_sbuf_tensor_at(name, shape, dt, offset=offset)

        def stack(top):
            def sb(name, shape, dt=F32):
                size = 4
                for n in shape[1:]:
                    size *= n
                t = place(name, shape, dt, top[0])
                top[0] += (size + 31) // 32 * 32
                return t
            return sb

        def sem(name):
            return ctx.enter_context(nc.semaphore(name))

        top = [(nc.sbuf_base + 31) // 32 * 32]
        sb = stack(top)
        xhi = sb("xhi", [P, KS, TOK], F32R)
        xlo = sb("xlo", [P, KS, TOK], F32R)
        ring0 = top[0]
        whi = [sb(f"whi{i}", [P, KS, P], F32R) for i in range(RING)]
        wlo = [sb(f"wlo{i}", [P, KS, P], F32R) for i in range(RING)]
        wraw = [sb(f"wraw{i}", [P, KS, P]) for i in range(2)]
        rms0 = top[0]
        rms = sb("rms", [P, TOK])
        cst = sb("cst", [P, 3 * P + (2 * LV - 1) * 64])
        ones = sb("ones", [P, P])
        ones_r = sb("ones_r", [P, P], F32R)
        prm = sb("prm", [P, 64])
        gb_col = sb("gb_col", [P, NT, 2, H])
        col = sb("col", [P, 64])
        ident, tri, pair_mask = cst[:, 0:P], cst[:, P:2 * P], cst[:, 2 * P:3 * P]
        inv_mask = cst[:, 3 * P:3 * P + (LV - 1) * 64].rearrange("p (l n) -> p l n", n=64)
        hg_mask = cst[:, 3 * P + (LV - 1) * 64:].rearrange("p (l n) -> p l n", n=64)
        nw, cw = prm[:, 0:KS], prm[:, 8:56].rearrange("p (c j) -> p c j", j=4)
        gnw, hnw, lbl = prm[:, 56:57], prm[:, 57:58], prm[:, 58:62]
        alog, dtb = prm[0:H, 62:63], prm[0:H, 63:64]
        eps, one = col[:, 0:1], col[:, 1:2]
        nega = col[0:H, 2:3]
        lb, omlb, lbe = col[:, 4:8], col[:, 8:12], col[:, 16:20]
        gcs, gle, kdc = col[:, 12:16], col[:, 16:20], col[:, 20:24]
        ssh, rh = col[:, 24:40].rearrange("p (t e) -> p t e", e=2), col[:, 40:48]

        arena = top[0]
        SLOT = 3 * HALF * 4
        X = place("X", [P, 9, 3 * HALF], F32, arena)
        xraw = place("xraw", [P, KS, TOK], F32, arena)
        work = arena + 56 * 1024

        w1 = [work]
        sb = stack(w1)
        pre = sb("pre", [P, 3 + TOK])
        conv = [sb(f"conv{i}", [P, HALF]) for i in range(2)]
        qkv_end = w1[0]
        sqx = [sb(f"sqx{i}", [P, TOK]) for i in range(2)]
        sqa = sb("sqa", [P, TOK])
        ab = sb("ab", [64, TOK])
        ab1 = sb("ab1", [H, TOK])
        ab2 = sb("ab2", [H, TOK])
        gb = sb("gb", [64, TOK])

        w2 = [work]
        sb = stack(w2)
        kdec = sb("kdec", [P, H, P])
        vtok = sb("vtok", [P, HALF])
        AT = sb("AT", [P, H, P])
        QK = sb("QK", [P, H, P])
        w2[0] = max(w2[0], qkv_end)
        sq = sb("sq", [P, 2, HALF])
        dec = [sb(f"dec{i}", [P, H, P]) for i in range(2)]
        egr = [sb(f"egr{i}", [P, H, P]) for i in range(2)]
        T = sb("T", [P, H, P])
        TT = sb("TT", [P, H, P])
        X0 = sb("X0", [P, HALF])
        vnew = sb("vnew", [P, H, P])
        S = sb("S", [P, H, P])
        U = [sb(f"U{i}", [P, H, P]) for i in range(1, LV)]

        w3 = [work]
        sb = stack(w3)
        hitok = sb("hitok", [P, NT, H, P])
        w3b = [w3[0]]
        hst = [sb(f"hst{i}", [P, HALF]) for i in range(2)]
        nrm = [sb(f"nrm{i}", [P, HALF]) for i in range(4)]
        sb = stack(w3b)
        HA = sb("HA", [P, H, P])
        kdt = sb("kdt", [P, H, P])
        HS = sb("HS", [P, H, P])
        TOT = sb("TOT", [P, H * P])
        KR1, FF1 = sb("KR1", [P, H, P]), sb("FF1", [P, H, P])
        assert w3b[0] >= w3[0]
        nrm_lo = [place(f"nrm_lo{i}", [P, HALF], F32R, w3b[0] + 2048 * i) for i in range(2)]
        QP = [sb(f"QP{i}", [P, H, P]) for i in range(2)]
        nrm_hi = [place(f"nrm_hi{i}", [P, HALF], F32R, w3b[0] + 2048 * i) for i in range(2)]
        KR = [sb("KR0", [P, H, P]), KR1]
        FF = [sb("FF0", [P, H, P]), FF1]
        zr = [sb(f"zr{i}", [P, HALF]) for i in range(2)]
        sg = [sb(f"sg{i}", [P, HALF]) for i in range(2)]

        yhi = [place("yahi", [P, H, TOK], F32R, work), place("ybhi", [P, H, TOK], F32R, arena + 4 * SLOT)]
        ylo = [place("yalo", [P, H, TOK], F32R, work + 16384),
               place("yblo", [P, H, TOK], F32R, arena + 4 * SLOT + 16384)]
        mat = [work + 32768, work + 36864] + [arena + 4096 * d for d in range(6)]
        merged = [place(f"merged{d}", [P, TOK], F32, mat[d]) for d in range(KS)]
        gateb = place("gateb", [P, TOK], F32, work + 40960)

        wohi = place("wohi", [P, KS, DM], F32R, work)
        wolo = place("wolo", [P, KS, DM], F32R, arena + 4 * SLOT)
        hat = [base + 4096 * k for base in (work, arena + 4 * SLOT) for k in range(RING)] + [rms0, work + 40960]
        hres = [place(f"hres{t}", [P, DM], F32, hat[t]) for t in range(NT)]
        scr = place("scr", [P, DM], F32, arena)
        fnw = place("fnw", [P, DM], F32, arena + 4096)
        assert max(w1[0], w2[0], w3b[0], work + 45056) <= nc.sbuf_usable_end

        B = [ctx.enter_context(nc.psum_tensor(f"bank{i}", [P, HALF], F32)) for i in range(8)]

        s_prm, s_cst, s_fn = sem("s_prm"), sem("s_cst"), sem("s_fn")
        s_x = [sem(f"x_landed{k}") for k in range(KS)]
        s_w = [sem("w_landed0"), sem("w_landed1")]
        s_res = [sem(f"res_landed{t}") for t in range(NT)]
        x_sq, x_hi, x_lo, sq_added = sem("x_sq"), sem("x_hi"), sem("x_lo"), sem("sq_added")
        ss_done, rms_done = sem("ss_done"), sem("rms_done")
        w_hi, w_lo = sem("w_hi"), sem("w_lo")
        acc_done = sem("acc_done")
        acc_out = [sem("acc_out0"), sem("acc_out1")]
        phase = sem("phase")
        setup, ones_ready = sem("setup"), sem("ones_ready")
        dstep, astep, pstep = sem("dstep"), sem("astep"), sem("pstep")
        tap_done, conv_done, silu_done = sem("tap_done"), sem("conv_done"), sem("silu_done")
        ab_row, ab_act, gb_row, gb_turned = sem("ab_row"), sem("ab_act"), sem("gb_row"), sem("gb_turned")
        sq_done, ssq_done, rs_done, qk_norm = sem("sq_done"), sem("ssq_done"), sem("rs_done"), sem("qk_norm")
        gcum_done, gcs_out, dif_done, kv_turned, att_done = (
            sem("gcum_done"), sem("gcs_out"), sem("dif_done"), sem("kv_turned"), sem("att_done"))
        dec_done, egr_done, kdc_done, v_out = sem("dec_done"), sem("egr_done"), sem("kdc_done"), sem("v_out")
        decm_done, kg_done = sem("decm_done"), sem("kg_done")
        tt_first, tt_turned, t_first = sem("tt_first"), sem("tt_turned"), sem("t_first")
        qk_ready, u_psum, u_ready, t_psum, t_ready = (
            sem("qk_ready"), sem("u_psum"), sem("u_ready"), sem("t_psum"), sem("t_ready"))
        tt_psum, tt_ready = sem("tt_psum"), sem("tt_ready")
        kd_ready = sem("kd_ready")
        ks_done, x0_done, tx_done, vn_done = sem("ks_done"), sem("x0_done"), sem("tx_done"), sem("vn_done")
        o_done, su_done, s_ready, oa_out = sem("o_done"), sem("su_done"), sem("s_ready"), sem("oa_out")
        hi_turned, hi_out = sem("hi_turned"), sem("hi_out")
        o_sq, o_hi, o_lo, o_ss, o_rs, o_nrm = sem("o_sq"), sem("o_hi"), sem("o_lo"), sem("o_ss"), sem("o_rs"), sem("o_nrm")
        hf_sig, hf_f, hk_lb, qf_done = sem("hf_sig"), sem("hf_f"), sem("hk_lb"), sem("qf_done")
        hd_psum, hl_psum, q_upd, k_upd = sem("hd_psum"), sem("hl_psum"), sem("q_upd"), sem("k_upd")
        hd_done, ha_done, tot_done = sem("hd_done"), sem("ha_done"), sem("tot_done")
        hk_turned, hk_out, ho_done, hs_done, hs_ready, ob_out = (
            sem("hk_turned"), sem("hk_out"), sem("ho_done"), sem("hs_done"), sem("hs_ready"), sem("ob_out"))
        z_sig, z_y = sem("z_sig"), sem("z_y")
        y_hi, y_lo = sem("y_hi"), sem("y_lo")
        g_sig, m_done = sem("g_sig"), sem("m_done")
        m_hi, m_lo = sem("m_hi"), sem("m_lo")
        out_done, h_res, h_rs, h_out = sem("out_done"), sem("h_res"), sem("h_rs"), sem("h_out")
        stored = sem("stored")

        def rows(t):
            return slice(P * t, P * (t + 1))

        def qkv(t):
            return X[:, t + 1, :].rearrange("p (c n) -> p c n", n=P)

        def blocks(ap, s):
            return ap.rearrange("p h (b e s) -> p (h b) e s", e=2, s=s)

        def packed(ap, s):
            return ap.rearrange("p (b s) -> p b s", s=s)

        def even_odd(ap, s):
            return ap.rearrange("p h (b e s) -> p h b e s", e=2, s=s)

        def mask(m, s):
            return m.rearrange("p (b s) -> p b s", s=s)[:, None, :, :].broadcast_to([P, 2, 64 // s, s])

        def pair(g):
            return slice(2 * g, 2 * g + 2)

        def by_head(ap):
            return ap[:, :, None].broadcast_to([P, H, P])

        def totals(lv, t, g=None):
            if lv == 0:
                tot = FF[t % 2][:].rearrange("p h n -> p (h n)")
            else:
                at = sum(H * P >> i for i in range(1, lv))
                tot = TOT[:, at:at + (H * P >> lv)]
            if g is not None:
                n = 2 * P >> lv
                tot = tot[:, n * g:n * (g + 1)]
            return tot.rearrange("p (b e) -> p b e", e=2)

        def level(t, lv, g):
            return (t * (LV - 1) + lv - 1) * 2 + g + 1

        def turned(t, lv, g):
            return (t * (LV - 2) + lv - 1) * 2 + g + 1

        def hlevel(t, lv, g):
            return (t * LV + lv) * 2 + g + 1

        def out_of_bank(eng, g):
            eng.wait_ge(acc_out[g % 2], g // 2 + 1)

        pieces_beside = ((0,), (1,), (2,), (3, 4), (5,), (6,), (7,), ())
        piece_at = (20, 30, 40, 50, 75, 85, 95, 105)
        pieces_inside = [[n for n in range(NT) if MM * u <= piece_at[n] < MM * (u + 1)] for u in range(NT)]

        def leave(eng):
            eng.drain().then_inc(phase, 1)

        def enter(eng, n):
            eng.wait_ge(phase, 4 * n)

        def wout(k):
            if k < RING:
                i = (S_OUT + k) % RING
                return [w[i][:].rearrange("p k n -> p (k n)") for w in (whi, wlo)]
            return wohi[:, k, :], wolo[:, k, :]

        block = ctx.enter_context(nc.Block())

        @block.sync
        def _(sp):
            def load_w(s):
                if s >= 2:
                    sp.wait_ge(w_hi, s - 1)
                    sp.wait_ge(w_lo, s - 1)
                sp.dma_start(wraw[s % 2][:].rearrange("p k n -> p (k n)"), w_tiles[s]).then_inc(s_w[s % 2], 16)

            sp.dma_start(prm[:], params).then_inc(s_prm, 16)
            sp.dma_start(xraw[:, 0, :], xT[0:P, :]).then_inc(s_x[0], 16)
            load_w(0)
            for k in range(1, KS):
                sp.dma_start(xraw[:, k, :], xT[P * k:P * (k + 1), :]).then_inc(s_x[k], 16)
                if k == 4:
                    load_w(1)
            sp.dma_start(cst[:], consts).then_inc(s_cst, 16)
            for s in range(2, NS):
                load_w(s)
            sp.wait_ge(acc_done, ALL_GROUPS)
            sp.wait_ge(m_done, 2 * KS)
            for t in range(NT):
                sp.dma_start(hres[t][:], xtok[rows(t), :]).then_inc(s_res[t], 16)
            sp.wait_ge(m_hi, KS)
            sp.wait_ge(m_lo, KS)
            sp.dma_start(fnw[:], fnorm).then_inc(s_fn, 16)
            for t in range(NT):
                sp.wait_ge(h_out, t + 1)
                sp.dma_start(out[rows(t), :], hres[t][:]).then_inc(stored, 16)
            sp.wait_ge(stored, 16 * NT)

        @block.tensor
        def _(pe):
            def gemm(s, n0=0, n1=2 * MM):
                for n in range(n0, n1):
                    half, m = divmod(n, MM)
                    k, term = divmod(m, 3)
                    g = first_group(s) + half
                    if n == 0:
                        pe.wait_ge(w_hi, s + 1)
                        pe.wait_ge(w_lo, s + 1)
                    if m == 0 and s > S_QKV:
                        pe.wait_ge(acc_out[g % 2], g // 2)
                    w = wlo if term == 2 else whi
                    x = xlo if term == 1 else xhi
                    mm = nc.tensor.matmul(B[g % 2][:], w[s % RING][:, k, :], x[:, k, HALF * half:HALF * (half + 1)],
                                          start=(m == 0), stop=(m == MM - 1))
                    if m == MM - 1:
                        mm.then_inc(acc_done, 1)

            def square_sums(src, banks):
                for i, b in enumerate(banks):
                    mm = nc.tensor.matmul(B[b][:], ones[:], src[:, i, :], start=True, stop=True)
                return mm

            def norm_sums(t):
                pe.wait_ge(sq_done, t + 1)
                if t:
                    pe.wait_ge(kd_ready, t)
                    pe.wait_ge(v_out, t)
                else:
                    pe.wait_ge(gb_turned, 2)
                nc.tensor.matmul(B[4][:], ones[:], sq[:, 1, :], start=True, stop=True).then_inc(ssq_done, 1)
                nc.tensor.matmul(B[2][:], ones[:], sq[:, 0, :], start=True, stop=True).then_inc(ssq_done, 1)

            def decay_sums(t):
                if t:
                    pe.wait_ge(s_ready, t)
                if t >= 2:
                    pe.wait_ge(oa_out, t - 1)
                nc.tensor.matmul(B[3][:, 0:H], tri, gb_col[:, t, 0, :], start=True, stop=True)
                for h in range(H):
                    mm = nc.tensor.matmul(B[5][:, P * h:P * (h + 1)],
                                          gb_col[:, t, 0, h:h + 1].broadcast_to([P, P]), tri, start=True, stop=True)
                mm.then_inc(gcum_done, 1)

            pe.wait_ge(setup, 1)
            pe.wait_ge(w_hi, 1)
            pe.wait_ge(w_lo, 1)
            for k in range(KS):
                pe.wait_ge(x_hi, k + 1)
                pe.wait_ge(x_lo, k + 1)
                for half in range(2):
                    part = slice(HALF * half, HALF * (half + 1))
                    for term in range(3):
                        w = wlo if term == 2 else whi
                        x = xlo if term == 1 else xhi
                        mm = nc.tensor.matmul(B[4 + half][:], w[0][:, k, :], x[:, k, part],
                                              start=(k == 0 and term == 0), stop=(k == KS - 1 and term == 2))
                    if k == KS - 1:
                        mm.then_inc(acc_done, 1)
            gemm(S_QKV, 0, 30)
            for half in range(2):
                pe.wait_ge(sq_added, KS - 1 + half)
                nc.tensor.matmul(B[2 + half][:], ones[:], sqa[:, HALF * half:HALF * (half + 1)],
                                 start=True, stop=True).then_inc(ss_done, 1)
            gemm(S_QKV, 30)
            for s in range(S_QKV + 1, S_HQF):
                for half in range(2):
                    gemm(s, MM * half, MM * (half + 1))
                    if s == S_QKV + 2 * H + 2 and half == 0:
                        norm_sums(0)
                        decay_sums(0)
                if s == 7:
                    pe.wait_ge(gb_row, 2)
                    pe.wait_ge(s_cst, 16)
                    for t in range(NT):
                        mm = nc.tensor.transpose(B[4][:, 64 * t:64 * (t + 1)], gb[:, P * t:P * (t + 1)],
                                                 ident[0:64, 0:64])
                    mm.then_inc(gb_turned, 1)
            leave(pe)

            fed = [0] * NT

            def fill(t, n, upto=2 * MM):
                n = min(n, upto - fed[t])
                gemm(S_HQF + t, fed[t], fed[t] + n)
                fed[t] += n

            def new_values(t):
                pe.wait_ge(x0_done, t + 1)
                pe.wait_ge(t_ready, level(t, LV - 1, 1))
                for h in range(H):
                    mm = nc.tensor.matmul(B[3][:, P * h:P * (h + 1)], TT[:, h, :], X0[:, P * h:P * (h + 1)],
                                          start=True, stop=True)
                mm.then_inc(tx_done, 1)

            def outputs(t):
                pe.wait_ge(vn_done, t + 1)
                if t < NT - 1:
                    pe.wait_ge(egr_done, t + 2)
                for h in range(H):
                    nc.tensor.matmul(B[5][:, P * h:P * (h + 1)], S[:, h, :], qkv(t)[:, h, :],
                                     start=True, stop=False)
                    mm = nc.tensor.matmul(B[5][:, P * h:P * (h + 1)], vnew[:, h, :], QK[:, h, :],
                                          start=False, stop=True)
                mm.then_inc(o_done, 1)
                for h in range(H):
                    mm = nc.tensor.matmul(B[3][:, P * h:P * (h + 1)], kdec[:, h, :], vnew[:, h, :],
                                          start=True, stop=True)
                mm.then_inc(su_done, 1)

            fill(0, 12)
            for t in range(NT):
                last = t == NT - 1
                upto = 2 * MM - (14 if last else 0)
                if t:
                    new_values(t - 1)
                pe.wait_ge(qk_norm, t + 1)
                for h in range(H):
                    both = X[:, t + 1, 0:2 * HALF].rearrange("p (g h n) -> p g h n", g=2, h=H)[:, :, h, :]
                    mm = nc.tensor.matmul(B[6 + h // 2][:, 256 * (h % 2):256 * (h % 2 + 1)],
                                          qkv(t)[:, H + h, :], both, start=True, stop=True)
                mm.then_inc(att_done, 1)
                pe.wait_ge(dif_done, t + 1)
                if t == 0:
                    pe.wait_ge(silu_done, 2 * (S_HQF - S_QKV))
                for i, b in ((1, 2), (2, 4)):
                    for h in range(H):
                        mm = nc.tensor.transpose(B[b][:, P * h:P * (h + 1)], qkv(t)[:, H * i + h, :], ident)
                mm.then_inc(kv_turned, 1)
                fill(t, 3)
                if t:
                    outputs(t - 1)
                fill(t, 6, upto)
                pe.wait_ge(tt_first, t + 1)
                pe.wait_ge(qk_ready, t + 1)
                for h in range(H):
                    mm = nc.tensor.transpose(B[6][:, P * h:P * (h + 1)], TT[:, h, :], ident)
                mm.then_inc(tt_turned, 1)
                fill(t, 3, upto)
                for lv in range(1, LV):
                    s = 1 << lv
                    for g in range(2):
                        if lv == 1:
                            pe.wait_ge(t_first, t + 1)
                        else:
                            pe.wait_ge(t_ready, level(t, lv - 1, g))
                        for i in range(2):
                            h = 2 * g + i
                            mm = nc.tensor.matmul(packed(B[6 + g][:, 64 * i:64 * (i + 1)], s), AT[:, h, :],
                                                  blocks(T[:, h:h + 1, :], s)[:, :, 0, :], start=True, stop=True)
                        mm.then_inc(u_psum, 1)
                        if lv > 1:
                            if lv == 2 and g == 0:
                                pe.wait_ge(s_ready, t + 1)
                            if lv == 3 and g == 0 and not last:
                                pe.wait_ge(gcs_out, t + 2)
                            if lv == 2 and g == 1 and not last:
                                pe.wait_ge(rs_done, 2 * t + 3)
                            for i in range(2):
                                mm = nc.tensor.transpose(B[3 + g][:, P * i:P * (i + 1)], T[:, 2 * g + i, :], ident)
                            mm.then_inc(tt_psum, 1)
                        fill(t, 1, upto)
                    for g in range(2):
                        pe.wait_ge(u_ready, level(t, lv, g))
                        if lv > 1:
                            pe.wait_ge(tt_ready, turned(t, lv - 1, g))
                        for i in range(2):
                            h = 2 * g + i
                            dst = packed(B[6 + g][:, 128 + 64 * i:128 + 64 * (i + 1)], s)
                            if lv < LV - 1:
                                mm = nc.tensor.matmul(dst, TT[:, h, :], blocks(U[lv - 1][:, h:h + 1, :], s)[:, :, 0, :],
                                                      start=True, stop=True)
                            else:
                                mm = nc.tensor.matmul(dst, U[lv - 1][:, h, :], blocks(TT[:, h:h + 1, :], s)[:, :, 1, :],
                                                      start=True, stop=True)
                        mm.then_inc(t_psum, 1)
                        fill(t, 2, upto)
                    if lv == 1 and not last:
                        norm_sums(t + 1)
                    if lv == 2 and not last:
                        decay_sums(t + 1)
                    if lv == 4:
                        pe.wait_ge(kg_done, 2 * (t + 1))
                        pe.wait_ge(s_ready, t + 1)
                        if last:
                            pe.wait_ge(kd_ready, t + 1)
                        else:
                            pe.wait_ge(rs_done, 2 * (t + 2))
                        for h in range(H):
                            mm = nc.tensor.matmul(B[2][:, P * h:P * (h + 1)], qkv(t)[:, H + h, :], S[:, h, :],
                                                  start=True, stop=True)
                        mm.then_inc(ks_done, 1)
                fill(t, 2 * MM, upto)
            fill(NT - 1, 2)
            new_values(NT - 1)
            fill(NT - 1, 6)
            outputs(NT - 1)
            fill(NT - 1, 2 * MM)
            leave(pe)

            pe.wait_ge(ones_ready, 1)

            def output_squares(n):
                pe.wait_ge(o_lo, n + 1)
                nc.tensor.matmul(B[4 + n % 4][:], ones_r[:], nrm_hi[n % 2][:], start=True, stop=False)
                nc.tensor.matmul(B[4 + n % 4][:], ones_r[:], nrm_lo[n % 2][:], start=False,
                                 stop=True).then_inc(o_ss, 1)

            for u in range(NT):
                for i, n in enumerate(pieces_beside[u]):
                    gemm(S_HI + u // 2, MM * (u % 2) + 18 * i, MM * (u % 2) + 18 + 6 * i)
                    output_squares(n)
                done = (0, 18, 24)[len(pieces_beside[u])]
                gemm(S_HI + u // 2, MM * (u % 2) + done, MM * (u % 2) + 24)
                if u >= 1:
                    turn_hi = u - 1
                    out_of_bank(pe, 2 * S_HI + turn_hi)
                    if turn_hi:
                        pe.wait_ge(hi_out, turn_hi)
                    for i in range(4):
                        mm = nc.tensor.transpose(B[2][:, P * i:P * (i + 1)], hst[turn_hi % 2][:, P * i:P * (i + 1)],
                                                 ident)
                    mm.then_inc(hi_turned, 1)
            gemm(S_ZA, 0, 12)
            out_of_bank(pe, 2 * S_HI + NT - 1)
            pe.wait_ge(hi_out, NT - 1)
            for i in range(4):
                mm = nc.tensor.transpose(B[2][:, P * i:P * (i + 1)], hst[(NT - 1) % 2][:, P * i:P * (i + 1)], ident)
            mm.then_inc(hi_turned, 1)
            leave(pe)

            for t in range(NT):
                fed = [MM * (t % 2) + (12 if t == 0 else 0)]

                def fill(n):
                    n = min(n, MM * (t % 2 + 1) - fed[0])
                    gemm(S_ZA + t // 2, fed[0], fed[0] + n)
                    fed[0] += n

                KRt, QPt = KR[t % 2], QP[t % 2]
                pe.wait_ge(hk_lb, t + 1)
                if t:
                    pe.wait_ge(ob_out, t)
                else:
                    pe.wait_ge(hi_out, NT)
                for h in range(H):
                    mm = nc.tensor.matmul(B[6][:, P * h:P * (h + 1)], KRt[:, h, :], X[:, h, P * t:P * (t + 1)],
                                          start=True, stop=True)
                mm.then_inc(hd_psum, 1)
                fill(1)
                for lv in range(LV):
                    s = 1 << lv
                    for g in range(2):
                        if lv == 0:
                            pe.wait_ge(qf_done, t + 1)
                        else:
                            pe.wait_ge(q_upd, hlevel(t, lv - 1, g))
                            pe.wait_ge(k_upd, hlevel(t, lv - 1, g))
                        if lv >= 2:
                            pe.wait_ge(ha_done, hlevel(t, lv - 2, g))
                        for i in range(2):
                            h = 2 * g + i
                            mm = nc.tensor.matmul(packed(B[2 + 2 * g + lv % 2][:, 64 * i:64 * (i + 1)], s),
                                                  KRt[:, h, :], blocks(QPt[:, h:h + 1, :], s)[:, :, 1, :],
                                                  start=True, stop=True)
                        mm.then_inc(hl_psum, 1)
                        fill(1 if lv in (2, 4, 6) else 2)
                fill(2)
                pe.wait_ge(k_upd, hlevel(t, LV - 1, 1))
                pe.wait_ge(hs_ready, t + 1)
                for h in range(H):
                    mm = nc.tensor.transpose(B[7][:, P * h:P * (h + 1)], KRt[:, h, :], ident)
                mm.then_inc(hk_turned, 1)
                fill(1)
                pe.wait_ge(q_upd, hlevel(t, LV - 1, 1))
                pe.wait_ge(ha_done, hlevel(t, LV - 1, 1))
                for h in range(H):
                    nc.tensor.matmul(B[6][:, P * h:P * (h + 1)], HS[:, h, :], QPt[:, h, :], start=True, stop=False)
                    mm = nc.tensor.matmul(B[6][:, P * h:P * (h + 1)], hitok[:, t, h, :], HA[:, h, :],
                                          start=False, stop=True)
                mm.then_inc(ho_done, 1)
                pe.wait_ge(hk_out, t + 1)
                for h in range(H):
                    mm = nc.tensor.matmul(B[7][:, P * h:P * (h + 1)], kdt[:, h, :], hitok[:, t, h, :],
                                          start=True, stop=True)
                mm.then_inc(hs_done, 1)
                fill(24)

            for u in range(NT):
                at = MM * (u % 2)
                for n in pieces_inside[u]:
                    upto = piece_at[n] - 2 * MM * (u // 2)
                    gemm(S_ZB + u // 2, at, upto)
                    at = upto
                    output_squares(NT + n)
                gemm(S_ZB + u // 2, at, MM * (u % 2 + 1))
            leave(pe)

            for d in range(KS):
                gemm(S_MERGE + 3 * d)
                gemm(S_MERGE + 3 * d + 1)
                s = S_MERGE + 3 * d + 2
                pe.wait_ge(w_hi, s + 1)
                pe.wait_ge(w_lo, s + 1)
                if d == 0:
                    pe.wait_ge(y_hi, 2 * H)
                    pe.wait_ge(y_lo, 2 * H)
                for half in range(2):
                    part = slice(HALF * half, HALF * (half + 1))
                    for br in range(2):
                        g = first_group(s) + 2 * half + br
                        pe.wait_ge(acc_out[g % 2], g // 2)
                        for h in range(H):
                            for term in range(3):
                                w = wlo if term == 2 else whi
                                y = ylo if term == 1 else yhi
                                mm = nc.tensor.matmul(B[g % 2][:], w[s % RING][:, H * br + h, :], y[br][:, h, part],
                                                      start=(h == 0 and term == 0),
                                                      stop=(h == H - 1 and term == 2))
                        mm.then_inc(acc_done, 1)

            def out_product(t, k, e, last):
                hi, lo = wout(k)
                for term in range(3):
                    m = xlo if term == 1 else xhi
                    w = lo if term == 2 else hi
                    mm = nc.tensor.matmul(B[t][:], m[:, k, P * t:P * (t + 1)], w[:, HALF * e:HALF * (e + 1)],
                                          start=(k == 0 and term == 0), stop=(k == KS - 1 and term == 2))
                if last:
                    mm.then_inc(out_done, 1)

            for k in range(KS):
                pe.wait_ge(m_hi, k + 1)
                pe.wait_ge(m_lo, k + 1)
                pe.wait_ge(w_hi, S_OUT + k + 1)
                pe.wait_ge(w_lo, S_OUT + k + 1)
                for t in (*range(2, NT), 0, 1):
                    if k == 0 and t < 2:
                        pe.wait_ge(acc_out[t], ALL_GROUPS // 2)
                    out_product(t, k, 0, k == KS - 1)
            for t in range(NT):
                pe.wait_ge(h_res, (t - 2) % NT + 1)
                for k in range(KS):
                    out_product(t, k, 1, k == KS - 1)

        def split_target(s):
            if s < S_OUT + RING:
                return whi[s % RING][:], wlo[s % RING][:]
            k = s - S_OUT
            cut = "p (k n) -> p k n"
            return wohi[:, k, :].rearrange(cut, k=KS), wolo[:, k, :].rearrange(cut, k=KS)

        def split_waits(eng, s):
            eng.wait_ge(s_w[s % 2], 16 * (s // 2 + 1))
            if s >= S_OUT + RING:
                eng.wait_ge(acc_done, ALL_GROUPS)
            elif s >= RING:
                eng.wait_ge(acc_done, end_group(s - RING))

        @block.scalar
        def _(act):
            def link(ins, n=[0]):
                n[0] += 1
                ins.then_inc(astep, 1)
                act.wait_ge(astep, n[0])

            def split_hi(s):
                split_waits(act, s)
                nc.scalar.activation(split_target(s)[0], wraw[s % 2][:], ACT.Identity).then_inc(w_hi, 1)

            nc.scalar.preload_act_table_set("natural_log_exp_and_others")
            act.wait_ge(setup, 1)
            nc.scalar.activation(ones_r[:], ones[:], ACT.Identity).then_inc(ones_ready, 1)
            act.wait_ge(s_prm, 16)

            def square_x(k):
                if k >= 2:
                    act.wait_ge(sq_added, k - 1)
                nc.scalar.activation(sqx[k % 2][:], xraw[:, k, :], ACT.Square).then_inc(x_sq, 1)

            for k in range(KS):
                act.wait_ge(s_x[k], 16)
                nc.scalar.activation(xhi[:, k, :], xraw[:, k, :], ACT.Identity, scale=nw[:, k:k + 1]).then_inc(x_hi, 1)
                if k == 0:
                    split_hi(0)
                elif k % 2 == 0:
                    square_x(k // 2 - 1)
            split_hi(1)
            for k in range(KS // 2 - 1, KS):
                square_x(k)
            for half in range(2):
                act.wait_ge(ss_done, half + 1)
                part = rms[:, HALF * half:HALF * (half + 1)]
                link(nc.scalar.activation(part, B[2 + half][:], ACT.Ln, bias=eps, scale=1.0 / DM))
                nc.scalar.activation(part, part, ACT.Exp, scale=-0.5).then_inc(rms_done, 1)
            nc.scalar.activation(nega, alog, ACT.Exp).then_inc(ab_act, 1)
            act.wait_ge(ab_row, 1)
            nc.scalar.activation(lbe, lbe, ACT.Exp).then_inc(ab_act, 1)
            split_hi(2)

            def squares(t):
                if t:
                    act.wait_ge(qk_norm, t)
                nc.scalar.activation(sq[:].rearrange("p g n -> p (g n)"), X[:, t + 1, 0:2 * HALF],
                                     ACT.Square).then_inc(sq_done, 1)

            def norm(t, i):
                act.wait_ge(ssq_done, 2 * (t + 1) - i)
                link(nc.scalar.activation(sq[:, i, :], B[2 + 2 * i][:], ACT.Ln, bias=eps))
                nc.scalar.activation(sq[:, i, :], sq[:, i, :], ACT.Exp, scale=-0.5).then_inc(rs_done, 1)

            def decays(t):
                act.wait_ge(dif_done, t + 1)
                nc.scalar.activation(dec[t % 2][:], dec[t % 2][:], ACT.Exp).then_inc(dec_done, 1)
                nc.scalar.activation(egr[t % 2][:].rearrange("p h n -> p (h n)"), B[5][:], ACT.Exp).then_inc(egr_done, 1)
                nc.scalar.activation(kdc, gle, ACT.Exp).then_inc(kdc_done, 1)

            def silu(u):
                s, half = S_QKV + u // 2, u % 2
                act.wait_ge(conv_done, u + 1)
                c = s - S_QKV
                dst = X[:, 4 * half + 1:4 * half + 5, P * c:P * (c + 1)]
                nc.scalar.activation(dst, conv[half][:].rearrange("p (t n) -> p t n", n=P),
                                     ACT.Silu).then_inc(silu_done, 1)

            for u in range(2 * (S_HQF - S_QKV)):
                c, half = divmod(u, 2)
                out_of_bank(act, 2 * S_QKV + u)
                if u >= 2:
                    act.wait_ge(silu_done, u - 1)
                nc.scalar.activation(conv[half][:], pre[:, HALF * half:HALF * (half + 1)], ACT.Identity,
                                     scale=cw[:, c, 0:1]).then_inc(tap_done, 1)
                if u:
                    silu(u - 1)
                if half:
                    split_hi(S_QKV + c + 2)
                if u == 4:
                    act.wait_ge(ab_row, 2)
                    link(nc.scalar.activation(ab2[:], ab2[:], ACT.Exp))
                    nc.scalar.activation(ab2[:], ab2[:], ACT.Ln, bias=one[0:H]).then_inc(ab_act, 1)
                    nc.scalar.activation(ab[32:32 + H, :], ab[32:32 + H, :], ACT.Exp, scale=-1.0).then_inc(ab_act, 1)
                if u == 2 * H * 2 + 3:
                    act.wait_ge(silu_done, 2 * H * 2)
                    act.wait_ge(sq_added, KS)
                    squares(0)
                elif u == 2 * H * 2 + 4:
                    norm(0, 1)
                    norm(0, 0)
                elif u == 2 * H * 2 + 6:
                    decays(0)
            silu(2 * (S_HQF - S_QKV) - 1)
            leave(act)
            enter(act, 1)

            nc.scalar.preload_act_table_set("natural_log_exp_and_others")

            def turned_t(t, lv):
                for g in range(2):
                    act.wait_ge(tt_psum, turned(t, lv, g))
                    nc.scalar.activation(TT[:, pair(g), :].rearrange("p h n -> p (h n)"), B[3 + g][:, 0:256],
                                         ACT.Identity).then_inc(tt_ready, 1)

            for t in range(NT + 1):
                if t < NT:
                    act.wait_ge(kv_turned, t + 1)
                    nc.scalar.activation(vtok[:], B[4][:], ACT.Identity).then_inc(v_out, 1)
                if t:
                    act.wait_ge(o_done, t)
                    nc.scalar.activation(X[:, t - 1, 2 * HALF:3 * HALF], B[5][:], ACT.Identity).then_inc(oa_out, 1)
                if t < NT:
                    act.wait_ge(tt_turned, t + 1)
                    nc.scalar.activation(T[:].rearrange("p h n -> p (h n)"), B[6][:], ACT.Identity).then_inc(t_first, 1)
                if t < NT - 1:
                    squares(t + 1)
                for lv in range(1, LV - 1 if t < NT else 1):
                    if lv == 1 and t < NT - 1:
                        norm(t + 1, 1)
                    turned_t(t, lv)
                    if lv == 1 and t < NT - 1:
                        norm(t + 1, 0)
                    if lv == 3:
                        split_hi(S_HQF + t + 2)
                    if lv == 4 and t < NT - 1:
                        decays(t + 1)
            leave(act)
            enter(act, 2)

            def out_squares(n):
                if n >= 4:
                    act.wait_ge(o_nrm, n - 3)
                u = n - NT
                src = X[:, n, 2 * HALF:3 * HALF] if n < NT else X[:, u // 2, HALF * (u % 2):HALF * (u % 2 + 1)]
                nc.scalar.activation(nrm[n % 4][:], src, ACT.Square).then_inc(o_sq, 1)
                act.wait_ge(o_sq, n + 1)
                nc.scalar.activation(nrm_hi[n % 2][:], nrm[n % 4][:], ACT.Identity).then_inc(o_hi, 1)

            def out_rms(n):
                act.wait_ge(o_ss, n + 1)
                r = nrm[n % 4][:]
                link(nc.scalar.activation(r, B[4 + n % 4][:], ACT.Ln, bias=eps, scale=1.0 / P))
                nc.scalar.activation(r, r, ACT.Exp, scale=-0.5).then_inc(o_rs, 1)

            def hi_copy(u):
                act.wait_ge(hi_turned, u + 1)
                c, half = divmod(u, 2)
                nc.scalar.activation(hitok[:, 4 * half:4 * half + 4, c, :],
                                     B[2][:].rearrange("p (t n) -> p t n", n=P), ACT.Identity).then_inc(hi_out, 1)

            def forget(t):
                tile = X[:, 4:8, P * t:P * (t + 1)]
                if t >= 2:
                    act.wait_ge(hk_turned, t - 1)
                nc.scalar.activation(FF[t % 2][:], tile, ACT.Sigmoid).then_inc(hf_sig, 1)
                nc.scalar.activation(KR[t % 2][:], tile, ACT.Sigmoid, scale=-1.0).then_inc(hf_sig, 1)
                act.wait_ge(hf_sig, 2 * (t + 1))
                for h in range(H):
                    f = FF[t % 2][:, h, :]
                    ins = nc.scalar.activation(f, f, ACT.Identity, bias=lb[:, h:h + 1], scale=omlb[:, h:h + 1])
                ins.then_inc(hf_f, 1)

            for n in range(2):
                out_squares(n)
            for u in range(NT):
                for n in pieces_beside[u]:
                    out_rms(n)
                    if n + 2 < NT:
                        out_squares(n + 2)
                if u in (1, 3, 5, 6):
                    split_hi(S_HI + (u + 4) // 2)
                if u == NT - 1:
                    forget(0)
                if u:
                    hi_copy(u - 1)
            hi_copy(NT - 1)
            leave(act)
            enter(act, 3)

            def z_gate(u):
                out_of_bank(act, 2 * S_ZA + u)
                nc.scalar.activation(sg[u % 2][:], zr[u % 2][:], ACT.Sigmoid).then_inc(z_sig, 1)

            for t in range(NT):
                if t < NT - 1:
                    forget(t + 1)
                if t:
                    z_gate(t - 1)
                if t % 2:
                    split_hi(S_ZA + t // 2 + 2)
                act.wait_ge(hk_turned, t + 1)
                nc.scalar.activation(kdt[:].rearrange("p h n -> p (h n)"), B[7][:], ACT.Identity).then_inc(hk_out, 1)
                act.wait_ge(ho_done, t + 1)
                nc.scalar.activation(X[:, 0:4, P * t:P * (t + 1)], B[6][:].rearrange("p (h n) -> p h n", n=P),
                                     ACT.Identity).then_inc(ob_out, 1)
            act.wait_ge(hs_ready, NT + 1)
            act.wait_ge(ob_out, NT)
            for n in range(2):
                out_squares(NT + n)
            z_gate(NT - 1)

            nc.scalar.preload_act_table_set("natural_log_exp_and_others")
            for n in range(NT):
                out_rms(NT + n)
                if n + 2 < NT:
                    out_squares(NT + n + 2)
                if n == 3:
                    split_hi(S_ZB + 2)
                    z_gate(NT)
                    z_gate(NT + 1)
                    nc.scalar.preload_act_table_set("natural_log_exp_and_others")
            split_hi(S_ZB + 3)
            for u in range(2, NT):
                z_gate(NT + u)
                if u in (3, 5):
                    split_hi(S_ZB + u // 2 + 3)
            leave(act)
            enter(act, 4)

            for h in range(H):
                nc.scalar.activation(yhi[0][:, h, :].rearrange("p (t n) -> p t n", n=P),
                                     X[:, 0:NT, 2 * HALF + P * h:2 * HALF + P * (h + 1)], ACT.Identity).then_inc(y_hi, 1)
            act.wait_ge(y_lo, H)
            for h in range(H):
                nc.scalar.activation(yhi[1][:, h, :], X[:, h, 0:TOK], ACT.Identity).then_inc(y_hi, 1)
            for d in range(KS):
                for r in range(2):
                    for half in range(2):
                        out_of_bank(act, first_group(S_MERGE + 3 * d + r) + half)
                        buf = (gateb if r else merged[d])[:, HALF * half:HALF * (half + 1)]
                        nc.scalar.activation(buf, buf, ACT.Sigmoid).then_inc(g_sig, 1)
                    split_hi(S_MERGE + 3 * d + r + 2)
                if d < KS - 1:
                    split_hi(S_MERGE + 3 * d + 4)
            act.wait_ge(acc_done, first_group(S_OUT - 1))
            for k in range(KS):
                act.wait_ge(m_done, 2 * (k + 1))
                nc.scalar.activation(xhi[:, k, :], merged[k][:], ACT.Identity).then_inc(m_hi, 1)
                if k == 3:
                    split_hi(S_OUT + 1)
            for k in range(2, KS):
                split_hi(S_OUT + k)
            nc.scalar.preload_act_table_set("natural_log_exp_and_others")
            for t in range(NT):
                act.wait_ge(h_res, NT + t + 1)
                link(nc.scalar.activation(scr[:], hres[t][:], ACT.Square, accum_out=ssh[:, t, 0:1]))
                link(nc.scalar.activation(rh[:, t:t + 1], ssh[:, t, 0:1], ACT.Ln, bias=eps, scale=1.0 / DM))
                nc.scalar.activation(rh[:, t:t + 1], rh[:, t:t + 1], ACT.Exp, scale=-0.5).then_inc(h_rs, 1)

        @block.gpsimd
        def _(pool):
            def split_lo(s):
                split_waits(pool, s)
                pool.wait_ge(w_hi, s + 1)
                hi, lo = split_target(s)
                nc.gpsimd.tensor_tensor(lo, wraw[s % 2][:], hi.bitcast(F32), ALU.subtract).then_inc(w_lo, 1)

            nc.gpsimd.memset(ones[:], 1.0)
            nc.gpsimd.memset(one, 1.0)
            nc.gpsimd.memset(eps, EPS).then_inc(setup, 1)
            for s in range(1, S_HQF + 1):
                split_lo(s)

            def mask_decays(t):
                pool.wait_ge(dec_done, t + 1)
                nc.gpsimd.tensor_tensor(dec[t % 2][:], dec[t % 2][:], tri[:, None, :].broadcast_to([P, H, P]),
                                        ALU.mult).then_inc(decm_done, 1)

            mask_decays(0)
            split_lo(S_HQF + 1)
            leave(pool)
            enter(pool, 1)
            for u in U:
                nc.gpsimd.memset(u[:], 0.0)
            nc.gpsimd.memset(S[:], 0.0).then_inc(s_ready, 1)
            for t in range(NT):
                pool.wait_ge(egr_done, t + 1)
                pool.wait_ge(kv_turned, t + 1)
                for i in (1, 0):
                    part = X[:, t + 1, HALF * i:HALF * (i + 1)]
                    nc.gpsimd.tensor_tensor(part, part, egr[t % 2][:].rearrange("p h n -> p (h n)"),
                                            ALU.mult).then_inc(kg_done, 1)
                split_lo(S_HQF + t + 2)
                if t < NT - 1:
                    mask_decays(t + 1)
            leave(pool)
            enter(pool, 2)
            def complement(t):
                pool.wait_ge(hf_sig, 2 * (t + 1))
                nc.gpsimd.tensor_tensor(KR[t % 2][:], KR[t % 2][:], by_head(omlb), ALU.mult).then_inc(hk_lb, 1)

            for u in range(NT):
                if u % 2:
                    split_lo(S_HI + u // 2 + 2)
            complement(0)
            leave(pool)
            enter(pool, 3)
            nc.gpsimd.memset(HS[:], 0.0).then_inc(hs_ready, 1)

            def z_apply(u):
                c, half = divmod(u % NT, 2)
                if u < NT:
                    o = X[:, 4 * half:4 * half + 4, 2 * HALF + P * c:2 * HALF + P * (c + 1)]
                else:
                    o = X[:, c, HALF * half:HALF * (half + 1)].rearrange("p (a b) -> p a b", b=P)
                pool.wait_ge(z_sig, u + 1)
                z3 = zr[u % 2][:].rearrange("p (a b) -> p a b", b=P)
                nc.gpsimd.tensor_tensor(z3, z3, sg[u % 2][:].rearrange("p (a b) -> p a b", b=P),
                                        ALU.mult).then_inc(pstep, 1)
                pool.wait_ge(pstep, u + 1)
                if u >= NT:
                    pool.wait_ge(o_nrm, u + 1)
                nc.gpsimd.tensor_tensor(o, o, z3, ALU.mult).then_inc(z_y, 1)

            for t in range(NT):
                pool.wait_ge(hf_f, t + 1)
                for lv in range(LV):
                    s = 1 << lv
                    if lv:
                        pool.wait_ge(tot_done, LV * t + lv)
                    for g in range(2):
                        pool.wait_ge(hl_psum, hlevel(t, lv, g))
                        k_even = blocks(KR[t % 2][:, pair(g), :], s)[:, :, 0, :]
                        nc.gpsimd.tensor_tensor(k_even, k_even,
                                                totals(lv, t, g)[:, :, 1:2].broadcast_to([P, 128 // s, s]),
                                                ALU.mult).then_inc(k_upd, 1)
                    if lv == 2 and t < NT - 1:
                        complement(t + 1)
                if t % 2:
                    split_lo(S_ZA + t // 2 + 2)
                if t:
                    z_apply(t - 1)
            z_apply(NT - 1)
            split_lo(S_ZB + 2)
            for u in range(NT):
                z_apply(NT + u)
                if u in (1, 3, 5):
                    split_lo(S_ZB + u // 2 + 3)
            leave(pool)
            enter(pool, 4)
            for s in range(S_MERGE + 2, NS):
                split_lo(s)

        @block.vector
        def _(dve):
            V = nc.vector
            steps = [0]

            def link(ins):
                steps[0] += 1
                ins.then_inc(dstep, 1)
                dve.wait_ge(dstep, steps[0])

            def take(g, dst, rows_=P):
                dve.wait_ge(acc_done, g + 1)
                half = g % 2
                r = rms[0:rows_, HALF * half:HALF * (half + 1)]
                b = B[half + (4 if g < 2 else 0)][0:rows_, :]
                if len(dst.shape) == 3:
                    r, b = (a.rearrange("p (t n) -> p t n", n=P) for a in (r, b))
                V.tensor_tensor(dst, b, r, ALU.mult).then_inc(acc_out[half], 1)

            dve.wait_ge(s_prm, 16)
            V.memset(pre[:, 0:3], 0.0)
            link(V.memset(gb[:], 0.0))
            V.tensor_tensor(lbe, lbl, lbl, ALU.subtract).then_inc(ab_row, 1)

            def add_square(k):
                dve.wait_ge(x_sq, k + 1)
                if k >= 2:
                    dve.wait_ge(sq_added, k - 1)
                for half in range(2 if k == KS - 1 else 1):
                    part = slice(HALF * half, HALF * (half + 1)) if k == KS - 1 else slice(0, TOK)
                    before = sqa if k >= 2 else sqx[0]
                    V.tensor_tensor(sqa[:, part], before[:, part], sqx[k % 2][:, part], ALU.add).then_inc(sq_added, 1)

            for k in range(KS):
                dve.wait_ge(x_hi, k + 1)
                V.scalar_tensor_tensor(out=xlo[:, k, :], in0=xraw[:, k, :], scalar=nw[:, k:k + 1],
                                       in1=xhi[:, k, :].bitcast(F32), op0=ALU.mult,
                                       op1=ALU.subtract).then_inc(x_lo, 1)
                if k == 0:
                    split_waits(dve, 0)
                    dve.wait_ge(w_hi, 1)
                    V.tensor_tensor(wlo[0][:], wraw[0][:], whi[0][:].bitcast(F32), ALU.subtract).then_inc(w_lo, 1)
                elif k >= 4 and k % 2 == 0:
                    add_square(k // 2 - 1)
            for k in range(KS // 2 - 1, KS):
                add_square(k)
            dve.wait_ge(rms_done, 2)
            take(0, ab[:, 0:HALF], 64)
            take(1, ab[:, HALF:TOK], 64)

            def decays(n):
                if n == 0:
                    dve.wait_ge(acc_out[0], 1)
                    dve.wait_ge(acc_out[1], 1)
                    V.tensor_scalar(ab1[:], ab[0:H, :], dtb, 0.0, ALU.add, ALU.max)
                    link(V.tensor_scalar(ab2[:], ab[0:H, :], dtb, None, ALU.add))
                    link(V.tensor_scalar(gb[0:H, :], ab2[:], -1.0, None, ALU.mult))
                    V.tensor_tensor(ab2[:], ab2[:], gb[0:H, :], ALU.min).then_inc(ab_row, 1)
                elif n == 1:
                    dve.wait_ge(ab_act, 1)
                    link(V.tensor_scalar(nega, nega, -1.0, None, ALU.mult))
                    dve.wait_ge(ab_act, 3)
                    link(V.tensor_tensor(ab1[:], ab1[:], ab2[:], ALU.add))
                    V.tensor_scalar(gb[0:H, :], ab1[:], nega, None, ALU.mult).then_inc(gb_row, 1)
                elif n == 2:
                    dve.wait_ge(ab_act, 4)
                    V.tensor_scalar(gb[32:32 + H, :], ab[32:32 + H, :], 1.0, None, ALU.add).then_inc(gb_row, 1)
                elif n == 3:
                    link(V.reciprocal(lb, lbe))
                    link(V.tensor_tensor(lbe, lbe, lb, ALU.mult))
                    link(V.tensor_tensor(lb, lbe, lbe, ALU.subtract))
                    V.tensor_scalar(omlb, lb, -1.0, 1.0, ALU.mult, ALU.add)
                elif n == 4:
                    dve.wait_ge(gb_turned, 1)
                    turned_gb = B[4][:].rearrange("p (t e n) -> p t e n", t=NT, n=32)[:, :, :, 0:H]
                    V.tensor_copy(gb_col[:, :, 0, :], turned_gb[:, :, 0, :])
                    V.reciprocal(gb_col[:, :, 1, :], turned_gb[:, :, 1, :]).then_inc(gb_turned, 1)

            decays_at = (3, 6, 7, 8, 15)

            def norm_q(t):
                dve.wait_ge(rs_done, 2 * t + 2)
                q = X[:, t + 1, 0:HALF]
                V.scalar_tensor_tensor(out=q, in0=q, scalar=QSCALE, in1=sq[:, 0, :], op0=ALU.mult,
                                       op1=ALU.mult).then_inc(qk_norm, 1)

            def norm_k(t):
                dve.wait_ge(rs_done, 2 * t + 1)
                k = X[:, t + 1, HALF:2 * HALF]
                V.tensor_tensor(k, k, sq[:, 1, :], ALU.mult)

            def differences(t, heads, last):
                dve.wait_ge(gcum_done, t + 1)
                if not last:
                    V.tensor_copy(gcs, B[3][:, 0:H]).then_inc(gcs_out, 1)
                    dve.wait_ge(gcs_out, t + 1)
                for h in heads:
                    V.tensor_scalar(dec[t % 2][:, h, :], B[5][:, P * h:P * (h + 1)], gcs[:, h:h + 1], 0.0,
                                    ALU.subtract, ALU.min)
                if last:
                    V.tensor_tensor(gle, B[5][:].rearrange("p (h n) -> p h n", n=P)[:, :, P - 1], gcs,
                                    ALU.subtract).then_inc(dif_done, 1)

            for u in range(2 * (S_HQF - S_QKV)):
                c, half = divmod(u, 2)
                if u:
                    dve.wait_ge(conv_done, u)
                take(2 * S_QKV + u, pre[:, 3 + HALF * half:3 + HALF * (half + 1)])
                dve.wait_ge(tap_done, u + 1)
                for j in range(1, 4):
                    ins = V.scalar_tensor_tensor(out=conv[half][:], in0=pre[:, HALF * half + j:HALF * (half + 1) + j],
                                                 scalar=cw[:, c, j:j + 1], in1=conv[half][:], op0=ALU.mult,
                                                 op1=ALU.add)
                    if j < 3:
                        link(ins)
                ins.then_inc(conv_done, 1)
                if u in decays_at:
                    decays(decays_at.index(u))
                if u == 2 * H * 2 + 5:
                    norm_k(0)
                    norm_q(0)
                    differences(0, (0, 1), False)
                elif u == 2 * H * 2 + 6:
                    differences(0, (2, 3), True)
            leave(dve)
            enter(dve, 1)

            def new_values(t):
                dve.wait_ge(tx_done, t + 1)
                V.tensor_tensor(vnew[:], B[3][:].rearrange("p (h n) -> p h n", n=P), by_head(gb_col[:, t, 1, :]),
                                ALU.mult).then_inc(vn_done, 1)

            def new_state(t):
                dve.wait_ge(su_done, t + 1)
                for h in range(H):
                    ins = V.scalar_tensor_tensor(out=S[:, h, :], in0=S[:, h, :], scalar=egr[t % 2][:, h, P - 1:P],
                                                 in1=B[3][:, P * h:P * (h + 1)], op0=ALU.mult, op1=ALU.add)
                ins.then_inc(s_ready, 1)

            for t in range(NT):
                if t:
                    new_values(t - 1)
                dve.wait_ge(att_done, t + 1)
                dve.wait_ge(decm_done, t + 1)
                for h in range(H):
                    ins = V.scalar_tensor_tensor(out=AT[:, h, :],
                                                 in0=B[6 + h // 2][:, 256 * (h % 2) + P:256 * (h % 2) + 2 * P],
                                                 scalar=gb_col[:, t, 1, h:h + 1], in1=dec[t % 2][:, h, :],
                                                 op0=ALU.mult, op1=ALU.mult)
                link(ins)
                link(V.tensor_tensor(TT[:], AT[:], pair_mask[:, None, :].broadcast_to([P, H, P]), ALU.mult))
                V.tensor_tensor(TT[:], TT[:], ident[:, None, :].broadcast_to([P, H, P]), ALU.add).then_inc(tt_first, 1)
                if t:
                    dve.wait_ge(o_done, t)
                for i in range(2):
                    ins = V.tensor_tensor(QK[:, 2 * i:2 * i + 2, :],
                                          B[6 + i][:].rearrange("p (h n) -> p h n", n=2 * P)[:, :, 0:P],
                                          dec[t % 2][:, 2 * i:2 * i + 2, :], ALU.mult)
                ins.then_inc(qk_ready, 1)
                if t:
                    new_state(t - 1)
                dve.wait_ge(kv_turned, t + 1)
                dve.wait_ge(kdc_done, t + 1)
                V.tensor_tensor(kdec[:], B[2][:].rearrange("p (h n) -> p h n", n=P), by_head(kdc),
                                ALU.mult).then_inc(kd_ready, 1)
                for lv in range(1, LV):
                    s = 1 << lv
                    if t == 0 and lv == 1:
                        dve.wait_ge(s_ready, 1)
                    for g in range(2):
                        dve.wait_ge(u_psum, level(t, lv, g))
                        V.tensor_tensor(even_odd(U[lv - 1][:, pair(g), :], s)[:, :, :, 0, :],
                                        B[6 + g][:, 0:128].rearrange("p (h b s) -> p h b s", h=2, s=s),
                                        mask(inv_mask[:, lv - 1, :], s), ALU.mult).then_inc(u_ready, 1)
                    for g in range(2):
                        dve.wait_ge(t_psum, level(t, lv, g))
                        if lv < LV - 1:
                            part = blocks(T[:, pair(g), :], s)[:, :, 0, :]
                        else:
                            part = blocks(TT[:, pair(g), :], s)[:, :, 1, :]
                        V.tensor_tensor(part, packed(B[6 + g][:, 128:256], s), part, ALU.add).then_inc(t_ready, 1)
                    if t < NT - 1:
                        if lv == 2:
                            differences(t + 1, (0, 1), False)
                        if lv == 3:
                            differences(t + 1, (2, 3), True)
                            norm_k(t + 1)
                        if lv == 4:
                            norm_q(t + 1)
                    if lv == 4:
                        take(2 * (S_HQF + t), X[:, t, 0:HALF])
                    if lv == 5:
                        dve.wait_ge(ks_done, t + 1)
                        dve.wait_ge(v_out, t + 1)
                        V.tensor_tensor(X0[:], vtok[:], B[2][:], ALU.subtract).then_inc(x0_done, 1)
                if t < NT - 1:
                    take(2 * (S_HQF + t) + 1, X[:, t, HALF:TOK])
            new_values(NT - 1)
            new_state(NT - 1)
            take(2 * (S_HQF + NT - 1) + 1, X[:, NT - 1, HALF:TOK])
            leave(dve)
            enter(dve, 2)

            def queries(t):
                if t >= 2:
                    dve.wait_ge(ho_done, t - 1)
                dve.wait_ge(hf_f, t + 1)
                V.tensor_tensor(QP[t % 2][:], X[:, 0:H, P * t:P * (t + 1)], FF[t % 2][:],
                                ALU.mult).then_inc(qf_done, 1)

            def squares_lo(n):
                dve.wait_ge(o_hi, n + 1)
                V.tensor_tensor(nrm_lo[n % 2][:], nrm[n % 4][:], nrm_hi[n % 2][:].bitcast(F32),
                                ALU.subtract).then_inc(o_lo, 1)

            squares_lo(0)
            squares_lo(1)
            for u in range(NT):
                if u >= 2:
                    dve.wait_ge(hi_turned, u - 1)
                take(2 * S_HI + u, hst[u % 2][:])
                for n in pieces_beside[u]:
                    dve.wait_ge(o_rs, n + 1)
                    o = X[:, n, 2 * HALF:3 * HALF]
                    V.scalar_tensor_tensor(out=o, in0=o, scalar=gnw, in1=nrm[n % 4][:], op0=ALU.mult,
                                           op1=ALU.mult).then_inc(o_nrm, 1)
                    if n + 2 < NT:
                        squares_lo(n + 2)
            queries(0)
            leave(dve)
            enter(dve, 3)

            def take_z(u):
                if u >= 2:
                    dve.wait_ge(z_y, u - 1)
                take(2 * S_ZA + u, zr[u % 2][:])

            def new_hstate(t, heads):
                dve.wait_ge(hs_done, t + 1)
                for h in heads:
                    ins = V.scalar_tensor_tensor(out=HS[:, h, :], in0=HS[:, h, :], scalar=TOT[:, 504 + h:505 + h],
                                                 in1=B[7][:, P * h:P * (h + 1)], op0=ALU.mult, op1=ALU.add)
                if H - 1 in heads:
                    ins.then_inc(hs_ready, 1)

            for t in range(NT):
                dve.wait_ge(hd_psum, t + 1)
                V.tensor_tensor(HA[:], B[6][:].rearrange("p (h n) -> p h n", n=P),
                                ident[:, None, :].broadcast_to([P, H, P]), ALU.mult).then_inc(hd_done, 1)
                for lv in range(LV):
                    s = 1 << lv
                    if lv:
                        dve.wait_ge(tot_done, LV * t + lv)
                    tot = totals(lv, t)
                    if lv == LV - 1:
                        dst = TOT[:, 504:508]
                    else:
                        dst = totals(lv + 1, t).rearrange("p b e -> p (b e)")
                    V.tensor_tensor(dst, tot[:, :, 0], tot[:, :, 1], ALU.mult).then_inc(tot_done, 1)
                    for g in range(2):
                        dve.wait_ge(hl_psum, hlevel(t, lv, g))
                        q_odd = blocks(QP[t % 2][:, pair(g), :], s)[:, :, 1, :]
                        V.tensor_tensor(q_odd, q_odd, totals(lv, t, g)[:, :, 0:1].broadcast_to([P, 128 // s, s]),
                                        ALU.mult).then_inc(q_upd, 1)
                    for g in range(2):
                        if lv:
                            dve.wait_ge(ha_done, hlevel(t, lv - 1, g))
                        else:
                            dve.wait_ge(hd_done, t + 1)
                        V.copy_predicated(even_odd(HA[:, pair(g), :], s)[:, :, :, 1, :],
                                          mask(hg_mask[:, lv, :].bitcast(I32), s),
                                          B[2 + 2 * g + lv % 2][:, 0:128].rearrange("p (h b s) -> p h b s", h=2, s=s)
                                          ).then_inc(ha_done, 1)
                    if lv in (1, 2) and t:
                        new_hstate(t - 1, range(2 * lv - 2, 2 * lv))
                    if lv == 4 and t < NT - 1:
                        queries(t + 1)
                    if lv == 5 and t:
                        take_z(t - 1)
            new_hstate(NT - 1, range(H))
            squares_lo(NT)
            squares_lo(NT + 1)
            take_z(NT - 1)

            for u in range(NT):
                for n in pieces_inside[u]:
                    dve.wait_ge(o_rs, NT + n + 1)
                    o = X[:, n // 2, HALF * (n % 2):HALF * (n % 2 + 1)]
                    V.scalar_tensor_tensor(out=o, in0=o, scalar=hnw, in1=nrm[n % 4][:], op0=ALU.mult,
                                           op1=ALU.mult).then_inc(o_nrm, 1)
                    if n + 2 < NT:
                        squares_lo(NT + n + 2)
                take_z(NT + u)
            leave(dve)
            enter(dve, 4)

            def split_y(br, h):
                dve.wait_ge(y_hi, H * br + h + 1)
                if br:
                    y, cut = X[:, h, 0:TOK], "p n -> p n"
                    hi, lo = yhi[br][:, h, :], ylo[br][:, h, :]
                else:
                    y = X[:, 0:NT, 2 * HALF + P * h:2 * HALF + P * (h + 1)]
                    hi, lo = (a[:, h, :].rearrange("p (t n) -> p t n", n=P) for a in (yhi[br], ylo[br]))
                V.tensor_tensor(lo, y, hi.bitcast(F32), ALU.subtract).then_inc(y_lo, 1)

            def split_merged(ks):
                for k in ks:
                    dve.wait_ge(m_hi, k + 1)
                    V.tensor_tensor(xlo[:, k, :], merged[k][:], xhi[:, k, :].bitcast(F32),
                                    ALU.subtract).then_inc(m_lo, 1)

            def take_gate(d, r, half):
                take(first_group(S_MERGE + 3 * d + r) + half,
                     (gateb if r else merged[d])[:, HALF * half:HALF * (half + 1)])

            for h in range(H):
                split_y(0, h)
            take_gate(0, 0, 0)
            for h in range(2):
                split_y(1, h)
            take_gate(0, 0, 1)
            for h in range(2, H):
                split_y(1, h)
            for d in range(KS):
                for r in range(2):
                    for half in range(2):
                        if d:
                            dve.wait_ge(m_done, 2 * d)
                        if d or r:
                            take_gate(d, r, half)
                if d == KS - 1:
                    dve.wait_ge(acc_done, first_group(S_OUT - 1))
                for half in range(2):
                    if d == KS - 1 and half:
                        split_merged(range(3))
                    part = slice(HALF * half, HALF * (half + 1))
                    dve.wait_ge(g_sig, 4 * (d + 1))
                    for br, gate in ((0, merged[d]), (1, gateb)):
                        g = first_group(S_MERGE + 3 * d + 2) + 2 * half + br
                        dve.wait_ge(acc_done, g + 1)
                        V.tensor_tensor(gate[:, part], B[g % 2][:], gate[:, part], ALU.mult).then_inc(acc_out[g % 2], 1)
                        out_of_bank(dve, g)
                    V.tensor_tensor(merged[d][:, part], merged[d][:, part], gateb[:, part],
                                    ALU.add).then_inc(m_done, 1)
            split_merged(range(3, KS))
            for e in range(2):
                for i, t in enumerate(range(NT) if e else (*range(2, NT), 0, 1)):
                    if e == 0:
                        dve.wait_ge(s_res[t], 16)
                    dve.wait_ge(out_done, NT * e + i + 1)
                    part = hres[t][:, HALF * e:HALF * (e + 1)]
                    V.tensor_tensor(part, B[t][:], part, ALU.add).then_inc(h_res, 1)
                    if e:
                        if t == 0:
                            dve.wait_ge(s_fn, 16)
                        dve.wait_ge(h_rs, t + 1)
                        V.scalar_tensor_tensor(out=hres[t][:], in0=hres[t][:], scalar=rh[:, t:t + 1], in1=fnw[:],
                                               op0=ALU.mult, op1=ALU.mult).then_inc(h_out, 1)


def level_masks():
    import numpy as np
    inv = np.zeros((P, LV - 1, 64), np.float32)
    hg = np.zeros((P, LV, 64), np.float32)
    for lv in range(LV):
        s = 1 << lv
        for c in range(64):
            first = c // s * 2 * s
            if lv:
                inv[first + s:first + 2 * s, lv - 1, c] = -1.0
            hg[first:first + s, lv, c] = 1.0
    pairs = np.zeros((P, P), np.float32)
    pairs[np.arange(0, P, 2), np.arange(1, P, 2)] = -1.0
    return pairs, inv.reshape(P, -1), hg.reshape(P, -1)


def kernel(**inputs):
    import numpy as np
    import concourse.bacc as bacc
    from concourse.bass_utils import run_bass_kernel_spmd

    a = {k: np.asarray(v) for k, v in inputs.items()}
    f = np.float32
    x = np.ascontiguousarray(a["x"][0])
    w_in = a["w_in"][0]
    qk, v, heads, wide = H * P, H * P, H, H * P
    cuts = np.cumsum([2 * qk + v, heads, heads, v, wide, wide, wide, wide])
    c_qkv, c_a, c_b, c_za, c_hq, c_hf, c_hi, c_zb, c_gate = np.split(w_in, cuts, axis=1)
    w_ab = np.zeros((DM, P), f)
    w_ab[:, 0:H], w_ab[:, 32:32 + H] = c_a, c_b
    gate_a, gate_b = np.split(c_gate, 2, axis=1)

    def tiles(w):
        return list(w.reshape(w.shape[0] // P, P, w.shape[1] // P, P).transpose(2, 1, 0, 3))

    order = [*tiles(w_ab), *tiles(c_qkv), *tiles(c_hq), *tiles(c_hf), *tiles(c_hi), *tiles(c_za), *tiles(c_zb)]
    branches = a["w_branch"][0].reshape(2 * H * P, DM)
    for g0, g1, br in zip(tiles(gate_a), tiles(gate_b), tiles(branches)):
        order += [g0, g1, br]
    order += list(a["w_out"][0].reshape(KS, P, KS, P))
    w_tiles = np.ascontiguousarray(np.stack(order)).reshape(NS, P, KS * P)

    params = np.zeros((P, 64), f)
    params[:, 0:KS] = a["norm_w"][0].reshape(KS, P).T
    params[:, 8:56] = a["conv_w"][0].reshape(4, 12, P).transpose(2, 1, 0).reshape(P, 48)
    params[:, 56], params[:, 57] = a["gdn_norm_w"][0], a["hg_norm_w"][0]
    params[:, 58:62] = a["hg_lb_logits"][0].reshape(H, P).T
    params[0:H, 62], params[0:H, 63] = a["a_log"][0], a["dt_bias"][0]
    consts = np.concatenate([np.eye(P, dtype=f), np.triu(np.ones((P, P), f)), *level_masks()], axis=1)

    nc = bacc.Bacc("TRN2", target_bir_lowering=False, num_devices=1)
    arrays = {"xT": np.ascontiguousarray(x.T), "xtok": x, "w_tiles": w_tiles, "params": params,
              "fnorm": np.ascontiguousarray(np.broadcast_to(a["final_norm_w"], (P, DM))), "consts": consts}
    aps = [nc.dram_tensor(n, v.shape, mybir.dt.from_np(v.dtype), kind="ExternalInput").ap()
           for n, v in arrays.items()]
    out = nc.dram_tensor("out", (TOK, DM), F32, kind="ExternalOutput").ap()
    bass_hybrid_gdn_hgrn2(nc, *aps, out)
    r = run_bass_kernel_spmd(nc, [arrays], core_ids=[0])
    return r.results[0]["out"].reshape(1, TOK, DM)
```
